# Optimizing a Trainium2 kernel written in Bass

```python
import math
import jax, jax.numpy as jnp
from jax import lax
import numpy as np

D_MODEL = 1024
BATCH = 1
SEQ = 256
DEPTH = 2

HG_HEADS = 4
HG_W = D_MODEL // 4
HG_DK = HG_W // HG_HEADS
ML_HEADS = 4
ML_W = D_MODEL // 4
ML_DH = ML_W // ML_HEADS
FX_HEADS = 8
FX_W = D_MODEL // 2
FX_DH = FX_W // FX_HEADS
D_MIX = HG_W + ML_W + FX_W
SPLIT_SIZES = (HG_W, HG_W, HG_W, HG_W, ML_W, ML_W, ML_W, ML_HEADS, ML_HEADS, ML_W, FX_W, FX_W, FX_W, FX_HEADS)
D_IN = 4 * HG_W + 4 * ML_W + 2 * ML_HEADS + 3 * FX_W + FX_HEADS
CONV_K = 4
CHUNK = 64
Q_BLOCK = 128
D_FF = ((8 * D_MODEL // 3 + 127) // 128) * 128
N_EXPERTS = 8
TOP_K = 2
D_FF_EXPERT = 7 * D_MODEL // 2
EXPERT_BLOCK = 256
N_DENSE = (DEPTH + 1) // 2
N_MOE = DEPTH // 2
EPS = 1e-6

kernel_name = "hymba_style_hgrn2_mlstm_fox_moe"

def rmsnorm(x, g):
    xf = x.astype(jnp.float32)
    y = xf * lax.rsqrt(jnp.mean(xf * xf, axis=-1, keepdims=True) + EPS)
    return (y * g.astype(jnp.float32)).astype(x.dtype)

def head_rmsnorm(o, gain, heads):
    B, S, W = o.shape
    of = o.reshape(B, S, heads, W // heads)
    of = of * lax.rsqrt(jnp.mean(of * of, axis=-1, keepdims=True) + EPS)
    return of.reshape(B, S, W) * gain.astype(jnp.float32)

def to_chunks(t, heads):
    B, S, W = t.shape
    return t.reshape(B, S // CHUNK, CHUNK, heads, W // heads).transpose(1, 0, 3, 2, 4)

def gate_chunks(t):
    B, S, H = t.shape
    return t.reshape(B, S // CHUNK, CHUNK, H).transpose(1, 0, 3, 2)

def from_chunks(t):
    NC, B, H, C, d = t.shape
    return t.transpose(1, 0, 3, 2, 4).reshape(B, NC * C, H * d)

def causal_conv(x, w):
    C = x.shape[-1]
    return lax.conv_general_dilated(x, w[:, None, :].astype(x.dtype), window_strides=(1,),
                                    padding=[(CONV_K - 1, 0)],
                                    dimension_numbers=('NWC', 'WIO', 'NWC'),
                                    feature_group_count=C)

def hgrn2_mixer(q, fz, i, g, lb, gain):
    f32 = jnp.float32
    B = q.shape[0]
    lb = lb.astype(f32)
    fz = fz.astype(f32)
    log_f = jnp.logaddexp(jnp.log(lb), jnp.log1p(-lb) + jax.nn.log_sigmoid(fz))
    k = (1.0 - lb) * jax.nn.sigmoid(-fz)
    qc = to_chunks(q.astype(f32), HG_HEADS)
    kc = to_chunks(k, HG_HEADS)
    vc = to_chunks(i.astype(f32), HG_HEADS)
    gc = to_chunks(log_f, HG_HEADS)
    mask = jnp.tril(jnp.ones((CHUNK, CHUNK), bool))[:, :, None]

    def step(S, xs):
        qb, kb, vb, gb = xs
        b = jnp.cumsum(gb, axis=2)
        diff = b[:, :, :, None, :] - b[:, :, None, :, :]
        decay = jnp.exp(jnp.where(mask, diff, -jnp.inf))
        scores = jnp.einsum('bhtd,bhsd,bhtsd->bhts', qb, kb, decay)
        o = (jnp.einsum('bhts,bhsv->bhtv', scores, vb)
             + jnp.einsum('bhtd,bhdv->bhtv', qb * jnp.exp(b), S))
        b_end = b[:, :, -1:, :]
        S = (jnp.exp(b_end[:, :, 0, :])[..., None] * S
             + jnp.einsum('bhsd,bhsv->bhdv', kb * jnp.exp(b_end - b), vb))
        return S, o

    S0 = jnp.zeros((B, HG_HEADS, HG_DK, HG_DK), f32)
    _, o = lax.scan(step, S0, (qc, kc, vc, gc))
    o = from_chunks(o)
    return head_rmsnorm(o, gain, HG_HEADS) * jax.nn.silu(g.astype(f32))

def mlstm_mixer(q, k, v, ig, fg, og, conv_w, b_i, b_f, gain):
    f32 = jnp.float32
    B = q.shape[0]
    qk = jax.nn.silu(causal_conv(jnp.concatenate([q, k], axis=-1), conv_w))
    q, k = jnp.split(qk.astype(f32), 2, axis=-1)
    k = k * (ML_DH ** -0.5)
    log_i = ig.astype(f32) + b_i.astype(f32)
    log_f = jax.nn.log_sigmoid(fg.astype(f32) + b_f.astype(f32))
    qc = to_chunks(q, ML_HEADS)
    kc = to_chunks(k, ML_HEADS)
    vc = to_chunks(v.astype(f32), ML_HEADS)
    ic = gate_chunks(log_i)
    fc = gate_chunks(log_f)
    mask = jnp.tril(jnp.ones((CHUNK, CHUNK), bool))

    def step(carry, xs):
        Cm, n, m = carry
        qb, kb, vb, lib, lfb = xs
        b = jnp.cumsum(lfb, axis=-1)
        d_log = jnp.where(mask, b[..., :, None] - b[..., None, :] + lib[..., None, :], -jnp.inf)
        inter = b + m[..., None]
        m_t = jnp.maximum(jnp.max(d_log, axis=-1), inter)
        w = jnp.einsum('bhtd,bhsd->bhts', qb, kb) * jnp.exp(d_log - m_t[..., None])
        s_inter = jnp.exp(inter - m_t)
        num = (jnp.einsum('bhts,bhsv->bhtv', w, vb)
               + s_inter[..., None] * jnp.einsum('bhtd,bhdv->bhtv', qb, Cm))
        den = w.sum(-1) + s_inter * jnp.einsum('bhtd,bhd->bht', qb, n)
        h = num / jnp.maximum(jnp.abs(den), jnp.exp(-m_t))[..., None]
        b_end = b[..., -1]
        log_w = b_end[..., None] - b + lib
        m_new = jnp.maximum(b_end + m, jnp.max(log_w, axis=-1))
        wk = jnp.exp(log_w - m_new[..., None])
        decay = jnp.exp(b_end + m - m_new)
        Cm = decay[..., None, None] * Cm + jnp.einsum('bhs,bhsd,bhsv->bhdv', wk, kb, vb)
        n = decay[..., None] * n + jnp.einsum('bhs,bhsd->bhd', wk, kb)
        return (Cm, n, m_new), h

    init = (jnp.zeros((B, ML_HEADS, ML_DH, ML_DH), f32),
            jnp.zeros((B, ML_HEADS, ML_DH), f32),
            jnp.zeros((B, ML_HEADS), f32))
    _, h = lax.scan(step, init, (qc, kc, vc, ic, fc))
    h = from_chunks(h)
    return head_rmsnorm(h, gain, ML_HEADS) * jax.nn.sigmoid(og.astype(f32))

def fox_mixer(q, k, v, fz, b_f):
    f32 = jnp.float32
    B, S, _ = q.shape

    def heads(t):
        return t.reshape(B, S, FX_HEADS, FX_DH).transpose(0, 2, 1, 3)

    q, k, v = heads(q), heads(k), heads(v)
    log_f = jax.nn.log_sigmoid(fz.astype(f32) + b_f.astype(f32)).transpose(0, 2, 1)
    c = jnp.cumsum(log_f, axis=-1)
    nb = S // Q_BLOCK
    q_blocks = q.reshape(B, FX_HEADS, nb, Q_BLOCK, FX_DH).transpose(2, 0, 1, 3, 4)
    c_blocks = c.reshape(B, FX_HEADS, nb, Q_BLOCK).transpose(2, 0, 1, 3)
    kpos = jnp.arange(S)
    scale = FX_DH ** -0.5

    def block(args):
        qb, cb, bi = args
        qpos = bi * Q_BLOCK + jnp.arange(Q_BLOCK)
        s = (jnp.einsum('bhqd,bhkd->bhqk', qb, k).astype(f32) * scale
             + cb[..., None] - c[:, :, None, :])
        s = jnp.where(kpos[None, :] <= qpos[:, None], s, -jnp.inf)
        p = jax.nn.softmax(s, axis=-1)
        return jnp.einsum('bhqk,bhkd->bhqd', p.astype(v.dtype), v)

    o = lax.map(block, (q_blocks, c_blocks, jnp.arange(nb)))
    o = o.transpose(1, 2, 0, 3, 4).reshape(B, FX_HEADS, S, FX_DH)
    return o.transpose(0, 2, 1, 3).reshape(B, S, FX_W)

def swiglu(h, w_gate, w_up, w_down):
    return (jax.nn.silu(h @ w_gate) * (h @ w_up)) @ w_down

def moe_swiglu(h, router, w_gate, w_up, w_down):
    B, S, D = h.shape
    N = B * S
    xt = h.reshape(N, D)
    logits = (xt @ router).astype(jnp.float32)
    top_val, top_idx = lax.top_k(logits, TOP_K)
    gates = jax.nn.softmax(top_val, axis=-1)
    A = N * TOP_K
    e_flat = top_idx.reshape(A)
    t_flat = jnp.repeat(jnp.arange(N, dtype=jnp.int32), TOP_K)
    g_flat = gates.reshape(A).astype(h.dtype)
    order = jnp.argsort(e_flat)
    e_s, t_s, g_s = e_flat[order], t_flat[order], g_flat[order]
    counts = jax.ops.segment_sum(jnp.ones((A,), jnp.int32), e_flat, num_segments=N_EXPERTS)
    starts = jnp.cumsum(counts) - counts
    padded = (counts + EXPERT_BLOCK - 1) // EXPERT_BLOCK * EXPERT_BLOCK
    pad_end = jnp.cumsum(padded)
    pad_start = pad_end - padded
    dest = pad_start[e_s] + (jnp.arange(A, dtype=jnp.int32) - starts[e_s])
    P = A + N_EXPERTS * EXPERT_BLOCK
    n_blocks = P // EXPERT_BLOCK
    tok_pad = jnp.full((P,), N, jnp.int32).at[dest].set(t_s)
    gate_pad = jnp.zeros((P,), h.dtype).at[dest].set(g_s)
    blk_expert = jnp.minimum(
        jnp.searchsorted(pad_end, jnp.arange(n_blocks) * EXPERT_BLOCK, side='right'),
        N_EXPERTS - 1)
    x_pad = jnp.concatenate([xt, jnp.zeros((1, D), h.dtype)], axis=0)

    def expert_block(args):
        tok, gt, e = args
        xb = x_pad[tok]
        hid = jax.nn.silu(xb @ w_gate[e]) * (xb @ w_up[e])
        return (hid @ w_down[e]) * gt[:, None]

    ys = lax.map(expert_block, (tok_pad.reshape(n_blocks, EXPERT_BLOCK),
                                gate_pad.reshape(n_blocks, EXPERT_BLOCK), blk_expert))
    y = jnp.zeros((N + 1, D), h.dtype).at[tok_pad].add(ys.reshape(P, D))
    return y[:N].reshape(B, S, D)

def setup_inputs(seed: int = 0) -> dict:
    key = jax.random.key(seed)
    ks = jax.random.split(key, 24)
    f32 = jnp.float32

    def nrm(k, shape, scale):
        return jax.random.normal(k, shape, f32) * scale

    return {
        "x": nrm(ks[0], (BATCH, SEQ, D_MODEL), 1.0),
        "attn_norm": 1.0 + nrm(ks[1], (DEPTH, D_MODEL), 0.02),
        "w_in": nrm(ks[2], (DEPTH, D_MODEL, D_IN), D_MODEL ** -0.5),
        "hgrn_lb": nrm(ks[3], (DEPTH, HG_W), 0.5),
        "hgrn_norm": 1.0 + nrm(ks[4], (DEPTH, HG_W), 0.02),
        "mlstm_conv": nrm(ks[5], (DEPTH, CONV_K, 2 * ML_W), CONV_K ** -0.5),
        "mlstm_b_i": nrm(ks[6], (DEPTH, ML_HEADS), 0.1),
        "mlstm_b_f": jnp.linspace(3.0, 6.0, ML_HEADS, dtype=f32)[None, :] + nrm(ks[7], (DEPTH, ML_HEADS), 0.1),
        "mlstm_norm": 1.0 + nrm(ks[8], (DEPTH, ML_W), 0.02),
        "fox_b_f": jnp.linspace(1.0, 6.0, FX_HEADS, dtype=f32)[None, :] + nrm(ks[9], (DEPTH, FX_HEADS), 0.1),
        "w_out": nrm(ks[10], (DEPTH, D_MIX, D_MODEL), D_MIX ** -0.5),
        "ffn_norm": 1.0 + nrm(ks[11], (DEPTH, D_MODEL), 0.02),
        "dense_w_gate": nrm(ks[12], (N_DENSE, D_MODEL, D_FF), D_MODEL ** -0.5),
        "dense_w_up": nrm(ks[13], (N_DENSE, D_MODEL, D_FF), D_MODEL ** -0.5),
        "dense_w_down": nrm(ks[14], (N_DENSE, D_FF, D_MODEL), D_FF ** -0.5),
        "router": nrm(ks[15], (N_MOE, D_MODEL, N_EXPERTS), D_MODEL ** -0.5),
        "moe_w_gate": nrm(ks[16], (N_MOE, N_EXPERTS, D_MODEL, D_FF_EXPERT), D_MODEL ** -0.5),
        "moe_w_up": nrm(ks[17], (N_MOE, N_EXPERTS, D_MODEL, D_FF_EXPERT), D_MODEL ** -0.5),
        "moe_w_down": nrm(ks[18], (N_MOE, N_EXPERTS, D_FF_EXPERT, D_MODEL), D_FF_EXPERT ** -0.5),
        "final_norm": 1.0 + nrm(ks[19], (D_MODEL,), 0.02),
    }

def reference(x, attn_norm, w_in, hgrn_lb, hgrn_norm, mlstm_conv, mlstm_b_i, mlstm_b_f,
              mlstm_norm, fox_b_f, w_out, ffn_norm, dense_w_gate, dense_w_up, dense_w_down,
              router, moe_w_gate, moe_w_up, moe_w_down, final_norm):
    lb_all = jnp.cumsum(jax.nn.softmax(hgrn_lb.astype(jnp.float32), axis=0), axis=0)
    lb_all = lb_all - lb_all[0:1]
    split_idx = np.cumsum(SPLIT_SIZES)[:-1].tolist()
    for l in range(DEPTH):
        h = rmsnorm(x, attn_norm[l])
        (hq, hf, hi, hg, mq, mk, mv, mi, mf, mo, fq, fk, fv, ff) = jnp.split(h @ w_in[l], split_idx, axis=-1)
        o_hg = hgrn2_mixer(hq, hf, hi, hg, lb_all[l], hgrn_norm[l])
        o_ml = mlstm_mixer(mq, mk, mv, mi, mf, mo, mlstm_conv[l], mlstm_b_i[l], mlstm_b_f[l], mlstm_norm[l])
        o_fx = fox_mixer(fq, fk, fv, ff, fox_b_f[l])
        mix = jnp.concatenate([o_hg.astype(x.dtype), o_ml.astype(x.dtype), o_fx.astype(x.dtype)], axis=-1)
        x = x + mix @ w_out[l]
        h = rmsnorm(x, ffn_norm[l])
        if l % 2 == 0:
            j = l // 2
            x = x + swiglu(h, dense_w_gate[j], dense_w_up[j], dense_w_down[j])
        else:
            j = l // 2
            x = x + moe_swiglu(h, router[j], moe_w_gate[j], moe_w_up[j], moe_w_down[j])
    return rmsnorm(x, final_norm)


_drawn_inputs = setup_inputs


def setup_inputs(seed=0):
    import zlib

    import numpy as np

    out = dict(_drawn_inputs(seed))
    spreads = {}
    factors = {'hgrn_norm': 7.991,
     'mlstm_b_i': 64.0,
     'mlstm_norm': 4.786,
     'final_norm': 22.561,
     'ffn_norm': 2.864}
    for name, (base, spread) in spreads.items():
        noise = np.random.default_rng([zlib.crc32(name.encode()), seed]).standard_normal(out[name].shape)
        drawn = base * np.exp(spread * noise) if base else spread * noise
        out[name] = __import__('jax').numpy.asarray(drawn.astype(out[name].dtype))
    for name, factor in factors.items():
        out[name] = (out[name] * factor).astype(out[name].dtype)
    return out
```

```python
from contextlib import ExitStack

import concourse.bass as bass
from concourse import mybir

P = 128
F32 = mybir.dt.float32
I32 = mybir.dt.int32
ALU = mybir.AluOpType
ACT = mybir.ActivationFunctionType
AX = mybir.AxisListType

EPS = 1e-6
BIG = 1e30
BANK = 512


def bass_hybrid_trunk_kernel(nc, x, attn_norm, w_in, hgrn_lb, hgrn_norm, mlstm_conv, mlstm_b_i,
                             mlstm_b_f, mlstm_norm, fox_b_f, w_out, ffn_norm, dense_w_gate,
                             dense_w_up, dense_w_down, router, moe_w_gate, moe_w_up, moe_w_down,
                             final_norm, out):
    _, SEQ, D = x.shape
    DEPTH = w_in.shape[0]
    T = SEQ // P
    KD = D // P
    HW = hgrn_norm.shape[1]
    FW = D - 2 * HW
    DH = 64
    NH = HW // DH
    NFH = FW // DH
    CK = mlstm_conv.shape[1]
    DFF = dense_w_gate.shape[2]
    NE = router.shape[2]
    FE = moe_w_gate.shape[3]
    assert (T, KD, HW, FW, DEPTH, NE, CK) == (2, 8, 256, 512, 2, 8, 4)
    SCALE = DH ** -0.5

    HQ0, HF0, HI0, HG0 = 0, HW, 2 * HW, 3 * HW
    MQ0 = 4 * HW
    MV0 = MQ0 + 2 * HW
    MI0 = MV0 + HW
    MO0 = MI0 + 2 * NH
    FQ0 = MO0 + HW
    FK0, FV0, FF0 = FQ0 + FW, FQ0 + 2 * FW, FQ0 + 3 * FW
    SLABS = [[(HF0, HW), (HQ0, HW)], [(MQ0, 2 * HW)], [(FQ0, FW)], [(FK0, FW)], [(FV0, FW)],
             [(MV0, HW), (MO0, HW)], [(HI0, 2 * HW)]]
    FEATURE_MAJOR = [True, True, True, True, False, False, False]
    NHALF = 2 * len(SLABS)
    STEPS = NHALF - 2
    LEVELS = 9

    SLOT = KD * BANK
    RING = 6
    ERING = RING + 1
    DCH = [(c, min(BANK, DFF - c)) for c in range(0, DFF, BANK)]
    ECH = [(c, BANK) for c in range(0, FE, BANK)]
    LAYER_UNITS = [len(SLABS) + 2 + 3 * len(DCH), len(SLABS) + 2]
    unit_base = [0, LAYER_UNITS[0]]
    UNITS = sum(LAYER_UNITS)
    JOB_UNITS = 3 * len(ECH)
    assert UNITS % RING == 0 and JOB_UNITS % ERING == 0
    LOADED = 32
    PER_JOB = JOB_UNITS // ERING
    uses_before = [UNITS // RING] * RING + [0]
    NCAND = 2 * NE

    with ExitStack() as ctx:
        def sb(name, shape, dt=F32):
            return ctx.enter_context(nc.sbuf_tensor(name, shape, dt))

        def sem(name):
            return ctx.enter_context(nc.semaphore(name))

        ps = [ctx.enter_context(nc.psum_tensor(f"bank{i}", [P, BANK], F32)) for i in range(8)]

        X = sb("X", [P, T, D])
        XN = sb("XN", [P, T, D])
        hT = sb("hT", [P, KD, SEQ])
        ring = sb("ring", [P, ERING * SLOT])
        last_slot = ring[:, RING * SLOT:ERING * SLOT]
        FQ = last_slot[:, 0:1024].rearrange("p (c t) -> p c t", c=4)
        FK = last_slot[:, 1024:2048].rearrange("p (c t) -> p c t", c=4)
        FV = last_slot[:, 2048:3072].rearrange("p (t n) -> p t n", t=T)
        PT = last_slot[:, 3072:4096]
        OM = last_slot[:, 0:1024].rearrange("p (t h d) -> p t h d", t=T, h=2 * NH)
        SQ = last_slot[:, 1024:2048].rearrange("p (t h d) -> p t h d", t=T, h=2 * NH)
        XNf = XN[:, :, :].rearrange("p t d -> p (t d)")
        FZ, TMP, LS, NK = (XNf[:, i * 512:(i + 1) * 512] for i in range(4))
        PP = [XNf[:, g * 1024:(g + 1) * 1024] for g in range(2)]
        HQ = sb("HQ", [P, 512])
        HK = sb("HK", [P, 512])
        LF = sb("LF", [P, 512])
        B = sb("B", [P, 512])
        DX = sb("DX", [P, 2, 512])
        QD = sb("QD", [P, 2, 512])
        KDk = sb("KDk", [P, 2, 512])
        SC = sb("SC", [P, 2, 4, P])
        SX = sb("SX", [P, 2, 2, P])
        HV = sb("HV", [P, T, HW])
        MC = sb("MC", [P, 4, SEQ])
        ER = sb("ER", [P, NH * 384])
        MR = ER[:, 0:4 * (SEQ + 3)].rearrange("p (c t) -> p c t", c=4)
        E = ER[:, :].rearrange("p (c q n) -> p c q n", c=2, q=2)
        VM = sb("VM", [P, T, NH, DH + 1])
        G2 = sb("G2", [P, T, 2 * NH, DH])
        mixT = sb("mixT", [P, KD, SEQ])

        ident = sb("ident", [P, P])
        UO = sb("UO", [P, 2 * P])
        NM = sb("NM", [P, P])
        MM = sb("MM", [P, 2 * P])
        LM = sb("LM", [P, 8, P])
        SEL = sb("SEL", [NH, NH, P])
        mhalf = sb("mhalf", [P, 2 * NH])
        PR = sb("PR", [68, P])
        PC = sb("PC", [P, 68])
        GB = sb("GB", [P, DEPTH, 16])
        HNG = sb("HNG", [P, DEPTH, 2 * HW])
        WG = sb("WG", [P, DEPTH, KD, 16])
        RW = sb("RW", [P, KD, NE])
        LB = sb("LB", [P, 5, 2])
        LBT = sb("LBT", [P, 4, 2])
        st = sb("st", [P, 2 * DEPTH + 1, 2, T])
        GA = sb("GA", [P, 4, T, 16])
        aa = sb("aa", [P, T, NH])
        bb = sb("bb", [P, T, NH])
        gT = sb("gT", [NH, SEQ])
        em = sb("em", [P, T, NH])
        nmx = sb("nmx", [P, 3, 8])
        rs = sb("rs", [P, 3, 2, 8])
        dn = sb("dn", [P, 2, T, NH])
        hs = sb("hs", [P, 2, T, 2 * NH])

        PCa = PC[:, 0:16].rearrange("p (l c) -> p l c", l=DEPTH)
        PCf = PC[:, 16:32].rearrange("p (l c) -> p l c", l=DEPTH)
        PCc = PC[:, 32:64].rearrange("p (l j c) -> p l j c", l=DEPTH, j=CK)
        PCl = PC[:, 64:68].rearrange("p (l c) -> p l c", l=DEPTH)

        SG = [XNf[:, i * 256:(i + 1) * 256] for i in range(4)]
        HT = [XNf[:, 1024 + i * 256:1280 + i * 256] for i in range(4)]
        xeT = MC[:, :, :].rearrange("p a b -> p (a b)").rearrange("p (c s) -> p c s", c=KD)
        hid = [HV[:, :, :].rearrange("p a b -> p (a b)"), HQ[:, :]]
        hidT = [HK[:, :], LF[:, :]]
        ye = mixT[:, 0:4, :].rearrange("p a b -> p (a b)")
        sil = [DX[:, 0, :], DX[:, 1, :]]
        selS = mixT[:, 4, :].rearrange("p (t s) -> p t s", t=T)
        selG = mixT[:, 5, :].rearrange("p (t s) -> p t s", t=T)
        selGT = mixT[:, 6, :]
        fgain = hT[:, 0:4, :].rearrange("p a b -> p (a b)")
        iota = sb("iota", [P, P])
        cidx = sb("cidx", [P, 2, 16])
        RT = sb("RT", [P, 12, 16])
        RV = sb("RV", [P, 8, T])
        RC = sb("RC", [P, 4, T, 16])
        OH = QD[:, 0, :].rearrange("p (i n) -> p i n", i=2)
        JB = sb("JB", [P, 5, 16])
        jobs = sb("jobs", [P, 32], I32)

        s_x = sem("x_loaded")
        s_par = sem("params_loaded")
        w_loaded = [sem(f"slot{i}_loaded") for i in range(ERING)]
        s_fg = sem("final_gain_loaded")
        s_out = sem("out_stored")
        s_cst = sem("consts_ready")
        s_prT = sem("param_rows_turned")
        s_pc = sem("param_cols_ready")
        s_lb = sem("lower_bound_steps")
        s_lba = sem("lower_bound_logs")
        s_ss = sem("square_sums")
        s_rms0 = sem("mean_squares")
        s_rms = sem("inv_rms")
        s_xn = sem("normalised")
        s_xt = sem("normalised_turned")
        s_hT = sem("hT_ready")
        s_res = sem("residual_added")
        s_gp = sem("gates_product")
        s_gv = sem("gate_values")
        s_ga = sem("gate_logs")
        s_ls = sem("gate_logsigmoids")
        s_cb = sem("mlstm_cumsum")
        s_a = sem("mlstm_a")
        s_aT = sem("mlstm_a_turned")
        s_g = sem("mlstm_running_max")
        s_gb = sem("mlstm_g_spread")
        s_m = sem("mlstm_m")
        s_em = sem("mlstm_floor")
        s_e0 = sem("mlstm_exponents")
        s_e = sem("mlstm_decays")
        s_pp = sem("projection_half")
        s_pe = sem("projection_evacuated")
        s_h1 = sem("hgrn_gate_logs")
        s_h2 = sem("hgrn_gate_sums")
        s_hk = sem("hgrn_keys")
        s_b = sem("hgrn_cumulated")
        s_d0 = sem("level_differences")
        s_dxa = sem("level_abs")
        s_dx = sem("level_decays")
        s_qd = sem("level_queries")
        s_kd = sem("level_keys")
        s_lp = sem("level_scores")
        s_lc = sem("level_copied")
        s_pad = sem("conv_padding")
        s_cv = sem("conv_steps")
        s_mc = sem("conv_silu")
        s_S = sem("attn_scores")
        s_mx = sem("attn_max")
        s_nx = sem("attn_neg_max")
        s_ex = sem("attn_exp")
        s_rr = sem("attn_inv_sum")
        s_pn = sem("attn_weights")
        s_tp = sem("attn_turned")
        s_te = sem("attn_turned_copied")
        s_pv = sem("attn_out")
        s_fo = sem("attn_out_copied")
        s_qk = sem("mlstm_scores")
        s_w = sem("mlstm_weights")
        s_ho = sem("hgrn_out")
        s_num = sem("mlstm_sums")
        s_oc = sem("hgrn_out_copied")
        s_dn = sem("mlstm_abs_den")
        s_dr = sem("mlstm_den_steps")
        s_oh = sem("mlstm_out")
        s_sq = sem("head_squares")
        s_hs = sem("head_square_sums")
        s_hr0 = sem("head_mean_squares")
        s_hr = sem("head_inv_rms")
        s_gr = sem("gate_activations")
        s_g2 = sem("gate_gain_steps")
        s_on = sem("heads_normalised")
        s_og = sem("heads_gated")
        s_mt = sem("mix_turned")
        s_me = sem("mix_turned_copied")
        s_wo = sem("out_projection")
        s_gu = sem("dense_gate_up")
        s_sg = sem("dense_silu")
        s_ht = sem("dense_hidden")
        s_dd = sem("dense_down")
        s_lg = sem("router_logits")
        s_rt = sem("routing_steps")
        s_rx = sem("routing_exp")
        s_rk = sem("routing_ranks")
        s_jl = sem("job_list")
        s_sel = sem("job_selection")
        s_gx = sem("job_gathered")
        s_xe = sem("job_tokens")
        s_sgT = sem("job_selection_turned")
        s_sgc = sem("job_selection_copied")
        s_eg = sem("expert_gate")
        s_eu = sem("expert_up")
        s_es = sem("expert_silu")
        s_eh = sem("expert_hidden")
        s_et = sem("expert_hidden_turned")
        s_ec = sem("expert_hidden_copied")
        s_ed = sem("expert_down")
        s_ey = sem("expert_out_copied")
        s_cz = sem("expert_combined")
        s_ca = sem("expert_added")
        s_me1 = sem("mix_turned_copied_tile1")
        s_gi = sem("mlstm_g_turned")
        s_fr = sem("residual_final")
        s_fin = sem("final_scaled")

        def halves(ap, k):
            return ap.rearrange("p (n m) -> p n m", m=2 ** k)

        consts = []
        NPAR = 16 * (4 + 5 * DEPTH + 2 * DEPTH + 1)
        RT_CHOSEN = 13
        RT_DIFF = RT_CHOSEN + 1

        block = ctx.enter_context(nc.Block())

        @block.sync
        def _(sp):
            sp.dma_start(X[:, :, :], x[0].rearrange("(t p) d -> p t d", p=P)).then_inc(s_x, 16)
            sp.dma_start(PR[0:16, :], attn_norm.rearrange("l (c p) -> (l c) p", p=P)).then_inc(s_par, 16)
            sp.dma_start(PR[16:32, :], ffn_norm.rearrange("l (c p) -> (l c) p", p=P)).then_inc(s_par, 16)
            sp.dma_start(PR[32:64, :], mlstm_conv.rearrange("l j (c p) -> (l j c) p", p=P)).then_inc(s_par, 16)
            sp.dma_start(PR[64:68, :], hgrn_lb.rearrange("l (c p) -> (l c) p", p=P)).then_inc(s_par, 16)
            for l in range(DEPTH):
                for src, c0, n in ((mlstm_b_i, 0, NH), (mlstm_b_f, NH, NH), (fox_b_f, 2 * NH, NFH)):
                    sp.dma_start(GB[:, l, c0:c0 + n], src[l:l + 1, :].to_broadcast([P, n])).then_inc(s_par, 16)
                wi = w_in[l].rearrange("(k p) n -> p k n", p=P)
                sp.dma_start(WG[:, l, :, 0:2 * NH], wi[:, :, MI0:MI0 + 2 * NH]).then_inc(s_par, 16)
                sp.dma_start(WG[:, l, :, 2 * NH:16], wi[:, :, FF0:FF0 + NFH]).then_inc(s_par, 16)

            def slot(s, k, n):
                return ring[:, s * SLOT:s * SLOT + k * n].rearrange("p (k n) -> p k n", k=k)

            released = {}

            def claim(u):
                if u - RING in released:
                    sp.wait_ge(*released[u - RING])
                return u % RING

            def columns(u, w, pieces):
                s, at = claim(u), 0
                wr = w.rearrange("(k p) n -> p k n", p=P)
                total = sum(n for _, n in pieces)
                for c0, n in pieces:
                    sp.dma_start(slot(s, KD, total)[:, :, at:at + n], wr[:, :, c0:c0 + n])\
                        .then_inc(w_loaded[s], LOADED // len(pieces))
                    at += n

            def rows(u, w, r0, n):
                s = claim(u)
                sp.dma_start(slot(s, n // P, D), w[r0:r0 + n, :].rearrange("(j p) n -> p j n", p=P))\
                    .then_inc(w_loaded[s], LOADED)

            for l in range(DEPTH):
                u = unit_base[l]
                for i, pieces in enumerate(SLABS):
                    columns(u + i, w_in[l], pieces)
                    released[u + i] = (s_pp, NHALF * l + 2 * i + 2)
                    if l == 0 and i == 0:
                        for ll in range(DEPTH):
                            sp.dma_start(HNG[:, ll, 0:HW], hgrn_norm[ll:ll + 1, :].to_broadcast([P, HW])).then_inc(s_par, 16)
                            sp.dma_start(HNG[:, ll, HW:], mlstm_norm[ll:ll + 1, :].to_broadcast([P, HW])).then_inc(s_par, 16)
                        sp.dma_start(RW[:, :, :], router[0].rearrange("(k p) e -> p k e", p=P)).then_inc(s_par, 16)
                u += len(SLABS)
                for n in range(2):
                    columns(u + n, w_out[l], [(n * BANK, BANK)])
                    released[u + n] = (s_wo, 4 * l + 2 * n + 2)
                u += 2
                if l == 0:
                    for c0, n in DCH:
                        columns(u, dense_w_gate[0], [(c0, n)])
                        columns(u + 1, dense_w_up[0], [(c0, n)])
                        rows(u + 2, dense_w_down[0], c0, n)
                        blocks = (c0 + n) // P
                        released[u] = released[u + 1] = (s_gu, blocks)
                        released[u + 2] = (s_dd, blocks)
                        u += 3

            def job_released(i, j):
                sp.wait_ge((s_eg, s_eu, s_ed)[i % 3], j * len(ECH) + i // 3 + 1)

            def job(j, e):
                for i in range(JOB_UNITS):
                    s = i % ERING
                    c0, n = ECH[i // 3]
                    if i >= ERING:
                        job_released(i - ERING, j)
                    elif not isinstance(j, int):
                        job_released(i + JOB_UNITS - ERING, j - 1)
                    elif s < RING:
                        claim(UNITS + s)
                    else:
                        sp.wait_ge(s_res, 12)
                    if i % 3 < 2:
                        w = (moe_w_gate, moe_w_up)[i % 3]
                        src = w[0, bass.ds(e, 1), :, c0:c0 + n].rearrange("o (k p) n -> p (o k) n", p=P)
                        dst = slot(s, KD, n)
                    else:
                        src = moe_w_down[0, bass.ds(e, 1), c0:c0 + n, :].rearrange("o (j p) n -> p (o j) n", p=P)
                        dst = slot(s, n // P, D)
                    sp.dma_start(dst, src).then_inc(w_loaded[s], LOADED)

            job(0, 0)
            sp.wait_ge(s_jl, 1)
            njobs = sp.value_load(jobs[0:1, 16:17], min_val=2, max_val=NCAND)
            with sp.Fori(1, njobs) as j:
                e = sp.value_load(jobs[0:1, bass.ds(j, 1)], min_val=0, max_val=NE - 1)
                job(j, e)
            sp.wait_ge(s_lg, 1)
            sp.dma_start(fgain, final_norm.rearrange("(a d) -> a d", a=1).to_broadcast([P, D])).then_inc(s_fg, 16)
            for t in range(T):
                sp.wait_ge(s_fin, t + 1)
                sp.dma_start(out[0, t * P:(t + 1) * P, :], XN[:, t, :]).then_inc(s_out, 16)
            sp.wait_ge(s_out, 16 * T)

        @block.gpsimd
        def _(pool):
            n = [0]

            def done(ins):
                ins.then_inc(s_cst, 1)
                n[0] += 1
                return n[0]

            def select(ap, op, pattern, base, mult, fill):
                pool.wait_ge(s_cst, n[0])
                done(pool.affine_select(out=ap, in_=ap, compare_op=op, fill=fill, base=base,
                                        pattern=pattern, channel_multiplier=mult))

            done(pool.memset(ident[:, :], 0.0))
            select(ident[:, :], ALU.not_equal, [[-1, P]], 0, 1, 1.0)
            done(pool.memset(UO[:, :], 1.0))
            select(UO[:, 0:P], ALU.is_ge, [[1, P]], 0, -1, 0.0)
            done(pool.memset(NM[:, :], 0.0))
            select(NM[:, :], ALU.is_ge, [[-1, P]], 0, 1, -BIG)
            done(pool.memset(MM[:, :], 0.0))
            select(MM[:, 0:P], ALU.is_ge, [[1, P]], 0, -1, -BIG)
            done(pool.memset(LM[:, :, :], 0.0))
            for k in range(1, 8):
                h = 2 ** (k - 1)
                v = halves(LM[:, k, :], k)[:, :, h:2 * h]
                pool.wait_ge(s_cst, n[0])
                done(pool.memset(v, 1.0))
                select(v, ALU.is_ge, [[-2 * h, P // (2 * h)], [0, h]], 0, 1, 0.0)
                select(v, ALU.is_ge, [[2 * h, P // (2 * h)], [0, h]], h - 1, -1, 0.0)
            pool.wait_ge(s_cst, n[0])
            done(pool.tensor_copy(LM[:, 0, :], ident[:, :]))
            done(pool.memset(SEL[:, :, :], 0.0))
            select(SEL[:, :, :], ALU.not_equal, [[-1, NH], [0, P]], 0, 1, -1.0)
            done(pool.memset(mhalf[:, :], -0.5))
            done(pool.memset(SC[:, :, :, :], 0.0))
            done(pool.memset(VM[:, :, :, DH:DH + 1], 1.0))
            done(pool.iota(iota[:, :], [[1, P]], base=0, channel_multiplier=0,
                           allow_small_or_imprecise_dtypes=True))
            done(pool.iota(cidx[:, 0, :], [[1, 16]], base=1, channel_multiplier=0,
                           allow_small_or_imprecise_dtypes=True))
            done(pool.iota(cidx[:, 1, :], [[1, NE], [0, 2]], base=0, channel_multiplier=0,
                           allow_small_or_imprecise_dtypes=True))
            nconst = n[0]
            consts.append(nconst)

            def inv_rms(i):
                pool.wait_ge(s_ss, 2 * i + 2)
                pool.tensor_scalar(st[:, i, 1, :], st[:, i, 0, :], 1.0 / D, EPS, ALU.mult, ALU.add).then_inc(s_rms0, 1)
                pool.wait_ge(s_rms0, i + 1)
                pool.tensor_tensor(st[:, i, 1, :], st[:, i, 1, :], mhalf[:, 0:T], ALU.pow).then_inc(s_rms, 1)

            for l in range(DEPTH):
                inv_rms(2 * l)
                if l:
                    pool.wait_ge(s_num, T * l)
                pool.memset(MR[:, :, 0:CK - 1], 0.0).then_inc(s_pad, 1)
                for k in range(1, LEVELS):
                    pool.wait_ge(s_dx, (LEVELS - 1) * l + k)
                    pool.wait_ge(s_hk, l + 1)
                    if k >= 3:
                        pool.wait_ge(s_lp, LEVELS * l + k - 1)
                    elif l:
                        pool.wait_ge(s_lp, LEVELS * l)
                    pool.tensor_tensor(KDk[:, k % 2, :], HK[:, :], DX[:, k % 2, :], ALU.mult).then_inc(s_kd, 1)
                pool.wait_ge(s_gr, l + 1)
                pool.tensor_scalar(G2[:, :, NH:, :], G2[:, :, NH:, :], 0.5, 0.5, ALU.mult, ALU.add).then_inc(s_g2, 1)
                pool.wait_ge(s_g2, 2 * l + 1)
                g2 = G2[:, :, :, :].rearrange("p t h d -> p t (h d)")
                pool.tensor_tensor(g2, g2, HNG[:, l, :].unsqueeze(1).to_broadcast([P, T, 2 * HW]), ALU.mult).then_inc(s_g2, 1)
                for t in range(T):
                    pool.wait_ge(s_hs, T * l + t + 1)
                    pool.tensor_scalar(hs[:, 1, t, :], hs[:, 0, t, :], 1.0 / DH, EPS, ALU.mult, ALU.add).then_inc(s_hr0, 1)
                    pool.wait_ge(s_hr0, T * l + t + 1)
                    pool.tensor_tensor(hs[:, 1, t, :], hs[:, 1, t, :], mhalf[:, :], ALU.pow).then_inc(s_hr, 1)
                inv_rms(2 * l + 1)
            inv_rms(2 * DEPTH)

        NCONST = consts[0]

        @block.scalar
        def _(act):
            def square_sums(i):
                if i == 0:
                    act.wait_ge(s_x, 16)
                elif i < 2 * DEPTH:
                    act.wait_ge(s_res, 4 * i)
                for t in range(T):
                    if i == 2 * DEPTH:
                        pass
                    act.activation(XN[:, t, :], X[:, t, :], ACT.Square, accum_out=st[:, i, 0, t:t + 1]).then_inc(s_ss, 1)

            def evacuate(l, i):
                act.wait_ge(s_pp, NHALF * l + i + 1)
                b = ps[i % 2]
                two = b[:, :].rearrange("p (c t) -> p c t", c=2)
                t = i % 2
                if i == 0:
                    act.copy(FZ, b[:, :]).then_inc(s_pe, 1)
                elif i == 1:
                    act.copy(HQ[:, :], b[:, :]).then_inc(s_pe, 1)
                elif i in (2, 3):
                    act.wait_ge(s_pad, l + 1)
                    act.copy(MR[:, 2 * t:2 * t + 2, CK - 1:], two).then_inc(s_pe, 1)
                elif i in (4, 5):
                    act.mul(FQ[:, 2 * t:2 * t + 2, :], two, SCALE).then_inc(s_pe, 1)
                elif i in (6, 7):
                    act.copy(FK[:, 2 * t:2 * t + 2, :], two).then_inc(s_pe, 1)
                elif i in (8, 9):
                    act.copy(FV[:, t, :], b[:, :]).then_inc(s_pe, 1)
                elif i in (10, 11):
                    act.copy(VM[:, t, :, 0:DH], b[:, 0:HW].rearrange("p (h d) -> p h d", h=NH))
                    act.copy(G2[:, t, NH:, :], b[:, HW:].rearrange("p (h d) -> p h d", h=NH)).then_inc(s_pe, 1)
                else:
                    act.copy(HV[:, t, :], b[:, 0:HW])
                    act.copy(G2[:, t, 0:NH, :], b[:, HW:].rearrange("p (h d) -> p h d", h=NH)).then_inc(s_pe, 1)

            def log1p_exp_neg_abs(dst, src, s, v, bias=None):
                if bias is None:
                    act.activation(dst, src, ACT.Abs).then_inc(s, 1)
                else:
                    for c in range(2):
                        ins = act.activation(dst[:, 256 * c:256 * c + 256], src[:, 256 * c:256 * c + 256], ACT.Abs,
                                             bias=bias[:, c:c + 1])
                    ins.then_inc(s, 1)
                act.wait_ge(s, v + 1)
                act.activation(dst, dst, ACT.Exp, scale=-1.0).then_inc(s, 1)
                act.wait_ge(s, v + 2)
                act.activation(dst, dst, ACT.Ln, bias=1.0).then_inc(s, 1)

            def attn_exp(l, g):
                act.wait_ge(s_nx, 3 * l + g + 1)
                n, w = (4, P) if g == 0 else (2, SEQ)
                if g == 2:
                    act.wait_ge(s_tp, 6 * l + 2)
                for p in range(2):
                    for c in range(n):
                        ins = act.activation(PP[g % 2][:, (p * n + c) * w:(p * n + c + 1) * w], ps[4 + p][:, c * w:(c + 1) * w],
                                             ACT.Exp, bias=nmx[:, g, p * n + c:p * n + c + 1],
                                             accum_out=rs[:, g, 0, p * n + c:p * n + c + 1])
                ins.then_inc(s_ex, 1)

            def attn_turned(l, g):
                for p in range(2):
                    act.wait_ge(s_tp, 6 * l + 2 * g + p + 1)
                    if g:
                        act.wait_ge(s_pv, 3 * l + g)
                    act.copy(PT[:, p * 512:p * 512 + 512], ps[6][:, :]).then_inc(s_te, 1)

            def attn_out(l, g):
                act.wait_ge(s_pv, 3 * l + g + 1)
                if g == 0:
                    act.copy(mixT[:, 4:8, 0:P], ps[7][:, :].rearrange("p (c t) -> p c t", c=4)).then_inc(s_fo, 1)
                else:
                    act.copy(mixT[:, 2 + 2 * g:4 + 2 * g, P:SEQ],
                             ps[7][:, 0:256].rearrange("p (c t) -> p c t", c=2)).then_inc(s_fo, 1)

            act.wait_ge(s_lb, 1)
            log1p_exp_neg_abs(LB[:, 1, :], LB[:, 0, :], s_lba, 0)

            for l in range(DEPTH):
                square_sums(2 * l)
                act.wait_ge(s_gv, l + 1)
                log1p_exp_neg_abs(GA[:, 3, :, :], GA[:, 0, :, :], s_ga, 3 * l)
                evacuate(l, 0)
                act.wait_ge(s_pe, NHALF * l + 1)
                h1 = 3 * l
                log1p_exp_neg_abs(TMP, FZ, s_h1, h1)
                evacuate(l, 1)
                act.wait_ge(s_h2, (2, 4)[l])
                if l == 0:
                    act.activation(HK[:, :], NK, ACT.Exp, scale=-1.0).then_inc(s_hk, 1)
                else:
                    for c in range(2):
                        ins = act.activation(HK[:, 256 * c:256 * c + 256], NK[:, 256 * c:256 * c + 256], ACT.Exp,
                                             scale=-1.0, bias=LB[:, 3, c:c + 1])
                    ins.then_inc(s_hk, 1)
                    log1p_exp_neg_abs(TMP, LS, s_h1, h1 + 3, bias=LB[:, 4, :])
                for k in range(STEPS):
                    if 1 <= k < LEVELS:
                        act.wait_ge(s_d0, (LEVELS - 1) * l + k)
                        act.activation(DX[:, k % 2, :], DX[:, k % 2, :], ACT.Abs).then_inc(s_dxa, 1)
                        act.wait_ge(s_dxa, (LEVELS - 1) * l + k)
                        act.activation(DX[:, k % 2, :], DX[:, k % 2, :], ACT.Exp, scale=-1.0).then_inc(s_dx, 1)
                    if k >= 8 and k - 8 < 3:
                        attn_exp(l, k - 8)
                    evacuate(l, k + 2)
                    if k == 3:
                        act.wait_ge(s_m, l + 1)
                        act.activation(em[:, :, :], bb[:, :, :], ACT.Exp, scale=-1.0).then_inc(s_em, 1)
                    if k == 5:
                        act.wait_ge(s_cv, 4 * CK * (l + 1))
                        act.activation(MC[:, :, :], MC[:, :, :], ACT.Silu).then_inc(s_mc, 1)
                    if k == 6:
                        act.wait_ge(s_e0, 8 * (l + 1))
                        act.activation(ER[:, :], ER[:, :], ACT.Exp).then_inc(s_e, 1)
                    if 9 <= k:
                        attn_out(l, k - 9)
                    if k >= 8 and k - 8 < 3:
                        attn_turned(l, k - 8)
                act.wait_ge(s_pe, NHALF * (l + 1))
                act.activation(G2[:, :, 0:NH, :], G2[:, :, 0:NH, :], ACT.Silu)
                act.activation(G2[:, :, NH:, :], G2[:, :, NH:, :], ACT.Tanh, scale=0.5).then_inc(s_gr, 1)
                act.wait_ge(s_ho, l + 1)
                act.copy(OM[:, :, 0:NH, :], ps[0][:, :].rearrange("p (t h d) -> p t h d", t=T, h=NH)).then_inc(s_oc, 1)
                for t in range(T):
                    act.wait_ge(s_num, T * l + t + 1)
                    act.activation(dn[:, 0, t, :], ps[1 + t][:, 0:NH * 65].rearrange("p (h e) -> p h e", h=NH)[:, :, DH],
                                   ACT.Abs).then_inc(s_dn, 1)
                act.wait_ge(s_oc, l + 1)
                for t in range(T):
                    act.wait_ge(s_oh, T * l + t + 1)
                    act.activation(SQ[:, t, :, :], OM[:, t, :, :], ACT.Square).then_inc(s_sq, 1)
                act.wait_ge(s_mt, T * l + 1)
                act.copy(mixT[:, 0:4, 0:P], ps[3][:, :].rearrange("p (c t) -> p c t", c=4)).then_inc(s_me, 1)

                square_sums(2 * l + 1)
                if l == 0:
                    for i in range(DFF // P):
                        act.wait_ge(s_gu, i + 1)
                        if i >= 4:
                            act.wait_ge(s_ht, i - 3)
                        act.activation(SG[i % 4], ps[i % 4][:, 0:SEQ], ACT.Silu).then_inc(s_sg, 1)

            act.wait_ge(s_rt, RT_DIFF)
            act.activation(RV[:, 3, :], RV[:, 2, :], ACT.Exp).then_inc(s_rx, 1)
            act.wait_ge(s_jl, 1)
            njobs = act.value_load(jobs[0:1, 16:17], min_val=2, max_val=NCAND)
            NCH = len(ECH)
            with act.Fori(0, njobs) as j:
                act.wait_ge(s_sgT, j + 1)
                act.copy(selGT, ps[4][:, 0:SEQ]).then_inc(s_sgc, 1)
                for c in range(NCH):
                    act.wait_ge(s_eg, j * NCH + c + 1)
                    if c >= 2:
                        act.wait_ge(s_eh, j * NCH + c - 1)
                    act.activation(sil[c % 2], ps[2 * (c % 2)][:, :], ACT.Silu).then_inc(s_es, 1)
                    if c >= 1:
                        act.wait_ge(s_et, j * NCH + c)
                        act.copy(hidT[(c - 1) % 2], ps[6][:, :]).then_inc(s_ec, 1)
                act.wait_ge(s_et, j * NCH + NCH)
                act.copy(hidT[(NCH - 1) % 2], ps[6][:, :]).then_inc(s_ec, 1)
                for n in range(2):
                    act.wait_ge(s_ed, j * NCH + NCH)
                    act.copy(ye[:, n * BANK:(n + 1) * BANK], ps[4 + n][:, :]).then_inc(s_ey, 1)
            act.wait_ge(s_fr, 1)
            square_sums(2 * DEPTH)

        @block.vector
        def _(dve):
            def bc(ap, shape):
                return ap.to_broadcast(shape)

            def normalise(i):
                dve.wait_ge(s_rms, i + 1)
                for t in range(T):
                    dve.tensor_scalar(XN[:, t, :], X[:, t, :], st[:, i, 1, t:t + 1], None, ALU.mult).then_inc(s_xn, 1)

            def turned(i, gain):
                for b in range(4):
                    t, c = b // 2, 4 * (b % 2)
                    dve.wait_ge(s_xt, 4 * i + b + 1)
                    dve.tensor_tensor(hT[:, c:c + 4, t * P:(t + 1) * P], ps[b][:, :].rearrange("p (c t) -> p c t", c=4),
                                      bc(gain[:, c:c + 4].unsqueeze(2), [P, 4, P]), ALU.mult).then_inc(s_hT, 1)

            def add_residual(ready):
                for n in range(2):
                    for t in range(T):
                        ready(n, t)
                        xs = X[:, t, n * BANK:(n + 1) * BANK]
                        dve.tensor_tensor(xs, xs, ps[4 + 2 * n + t][:, :], ALU.add).then_inc(s_res, 1)

            def level_difference(l, k):
                if k >= 3:
                    dve.wait_ge(s_kd, (LEVELS - 1) * l + k - 2)
                elif l:
                    dve.wait_ge(s_kd, (LEVELS - 1) * l)
                d = DX[:, k % 2, :]
                if k < 8:
                    v, h = halves(B[:, :], k), 2 ** (k - 1)
                    dve.tensor_tensor(halves(d, k), v, bc(v[:, :, h - 1:h], [P, 512 // (2 * h), 2 * h]), ALU.subtract)\
                        .then_inc(s_d0, 1)
                else:
                    v = B[:, :].rearrange("p (c t s) -> p c t s", c=2, t=T)
                    w = d.rearrange("p (c t s) -> p c t s", c=2, t=T)
                    dve.tensor_tensor(w[:, :, 0, :], v[:, :, 0, :], bc(v[:, :, 0, P - 1:P], [P, 2, P]), ALU.subtract)
                    dve.tensor_copy(w[:, :, 1, :], v[:, :, 1, :]).then_inc(s_d0, 1)

            def level_queries(l, k):
                dve.wait_ge(s_dx, (LEVELS - 1) * l + k)
                if k >= 3:
                    dve.wait_ge(s_lp, LEVELS * l + k - 1)
                dve.tensor_tensor(QD[:, k % 2, :], HQ[:, :], DX[:, k % 2, :], ALU.mult).then_inc(s_qd, 1)

            def level_copy(l, k):
                dve.wait_ge(s_lp, LEVELS * l + k + 1)
                for p in range(2):
                    if k < 8:
                        ins = dve.copy_predicated(SC[:, p, :, :], bc(LM[:, k, :].bitcast(I32).unsqueeze(1), [P, 4, P]),
                                                  ps[2 + p][:, :].rearrange("p (b t) -> p b t", b=4))
                    else:
                        ins = dve.tensor_copy(SX[:, p, :, :], ps[2 + p][:, 0:256].rearrange("p (c t) -> p c t", c=2))
                ins.then_inc(s_lc, 1)

            def attn_max(l, g):
                n, w = (4, P) if g == 0 else (2, SEQ)
                dve.wait_ge(s_S, 3 * l + g + 1)
                for p in range(2):
                    ins = dve.tensor_reduce(nmx[:, g, p * n:(p + 1) * n], ps[4 + p][:, :].rearrange("p (c s) -> p c s", c=n),
                                            AX.X, ALU.max)
                ins.then_inc(s_mx, 1)
                dve.wait_ge(s_mx, 3 * l + g + 1)
                dve.tensor_scalar(nmx[:, g, 0:2 * n], nmx[:, g, 0:2 * n], -1.0, None, ALU.mult).then_inc(s_nx, 1)

            def attn_weights(l, g):
                n, w = (8, P) if g == 0 else (4, SEQ)
                dve.wait_ge(s_ex, 3 * l + g + 1)
                dve.reciprocal(rs[:, g, 1, 0:n], rs[:, g, 0, 0:n]).then_inc(s_rr, 1)
                dve.wait_ge(s_rr, 3 * l + g + 1)
                v = PP[g % 2].rearrange("p (m w) -> p m w", m=n)
                dve.tensor_tensor(v, v, bc(rs[:, g, 1, 0:n].unsqueeze(2), [P, n, w]), ALU.mult).then_inc(s_pn, 1)

            def convolve(l):
                dve.wait_ge(s_pe, NHALF * l + 4)
                dve.wait_ge(s_pad, l + 1)
                for j in range(CK):
                    if j:
                        dve.wait_ge(s_cv, 4 * (CK * l + j))
                    for c in range(4):
                        w = PCc[:, l, j, c:c + 1]
                        if j == 0:
                            ins = dve.tensor_scalar(MC[:, c, :], MR[:, c, 0:SEQ], w, None, ALU.mult)
                        else:
                            ins = dve.scalar_tensor_tensor(out=MC[:, c, :], in0=MR[:, c, j:j + SEQ], scalar=w,
                                                           in1=MC[:, c, :], op0=ALU.mult, op1=ALU.add)
                        ins.then_inc(s_cv, 1)

            dve.wait_ge(s_prT, 1)
            dve.tensor_copy(PC[:, :], ps[6][:, 0:68]).then_inc(s_pc, 1)
            dve.wait_ge(s_pc, 1)
            dve.tensor_tensor(LB[:, 0, :], PCl[:, 1, :], PCl[:, 0, :], ALU.subtract).then_inc(s_lb, 1)
            dve.wait_ge(s_lba, 3)
            dve.wait_ge(s_lb, 1)
            dve.scalar_tensor_tensor(out=LB[:, 2, :], in0=LB[:, 0, :], scalar=0.0, in1=LB[:, 1, :],
                                     op0=ALU.min, op1=ALU.subtract).then_inc(s_lb, 1)
            dve.scalar_tensor_tensor(out=LBT[:, 0, :], in0=LB[:, 0, :], scalar=0.0, in1=LB[:, 1, :],
                                     op0=ALU.max, op1=ALU.add).then_inc(s_lb, 1)
            dve.wait_ge(s_lb, 3)
            dve.tensor_scalar(LB[:, 3, :], LBT[:, 0, :], -1.0, None, ALU.mult).then_inc(s_lb, 1)
            dve.wait_ge(s_lb, 4)
            dve.tensor_tensor(LB[:, 4, :], LB[:, 3, :], LB[:, 2, :], ALU.subtract).then_inc(s_lb, 1)

            for l in range(DEPTH):
                normalise(2 * l)
                turned(2 * l, PCa[:, l, :])
                dve.wait_ge(s_par, NPAR)
                dve.wait_ge(s_gp, l + 1)
                dve.tensor_tensor(GA[:, 0, :, :], ps[7][:, 0:32].rearrange("p (t g) -> p t g", t=T),
                                  bc(GB[:, l, :].unsqueeze(1), [P, T, 16]), ALU.add).then_inc(s_gv, 1)
                dve.wait_ge(s_gv, l + 1)
                dve.wait_ge(s_ga, 3 * l + 3)
                dve.scalar_tensor_tensor(out=GA[:, 1, :, :], in0=GA[:, 0, :, :], scalar=0.0, in1=GA[:, 3, :, :],
                                         op0=ALU.min, op1=ALU.subtract).then_inc(s_ls, 1)
                dve.wait_ge(s_ls, 2 * l + 1)
                dve.tensor_scalar(GA[:, 2, :, :], GA[:, 1, :, :], -1.0, None, ALU.mult).then_inc(s_ls, 1)
                dve.wait_ge(s_h1, 3 * l + 3)
                dve.wait_ge(s_pe, NHALF * l + 1)
                h2 = 2 * l
                dve.scalar_tensor_tensor(out=LS, in0=FZ, scalar=0.0, in1=TMP, op0=ALU.min, op1=ALU.subtract).then_inc(s_h2, 1)
                dve.scalar_tensor_tensor(out=NK, in0=FZ, scalar=0.0, in1=TMP, op0=ALU.max, op1=ALU.add).then_inc(s_h2, 1)
                lf = LS
                if l:
                    dve.wait_ge(s_h2, h2 + 2)
                    dve.wait_ge(s_lb, 5)
                    for c in range(2):
                        dve.tensor_scalar(FZ[:, 256 * c:256 * c + 256], LS[:, 256 * c:256 * c + 256], LB[:, 3, c:c + 1],
                                          LB[:, 2, c:c + 1], ALU.add, ALU.max).then_inc(s_h2, 1)
                    dve.wait_ge(s_h2, h2 + 4)
                    dve.wait_ge(s_h1, 9)
                    dve.tensor_tensor(LF[:, :], FZ, TMP, ALU.add).then_inc(s_h2, 1)
                    lf = LF[:, :]
                    dve.wait_ge(s_h2, h2 + 5)
                else:
                    dve.wait_ge(s_h2, 2)
                for c in range(4):
                    v = slice(c * P, (c + 1) * P)
                    dve.tensor_tensor_scan(B[:, v], lf[:, v], MM[:, P:2 * P], 0.0, ALU.add, ALU.add).then_inc(s_b, 1)
                dve.wait_ge(s_b, 4 * l + 4)
                dve.wait_ge(s_cb, l + 1)
                cb = ps[7][:, 32:40].rearrange("p (t h) -> p t h", t=T)
                dve.tensor_tensor(aa[:, :, :], GA[:, 0, :, 0:NH], cb, ALU.subtract).then_inc(s_a, 1)
                dve.tensor_copy(bb[:, :, :], cb).then_inc(s_a, 1)
                dve.wait_ge(s_aT, l + 1)
                for t in range(T):
                    v = slice(t * P, (t + 1) * P)
                    if t:
                        dve.wait_ge(s_g, T * l + t)
                    dve.tensor_tensor_scan(gT[:, v], ps[7][0:NH, 64 + t * P:64 + (t + 1) * P], MM[0:NH, P:2 * P],
                                           0.0 if t == 0 else gT[:, t * P - 1:t * P], ALU.max, ALU.max).then_inc(s_g, 1)

                for k in range(STEPS):
                    if 1 <= k < LEVELS:
                        level_difference(l, k)
                        level_queries(l, k)
                    if k == 3:
                        dve.wait_ge(s_gi, l + 1)
                        dve.wait_ge(s_a, 2 * l + 2)
                        dve.tensor_tensor(bb[:, :, :], bb[:, :, :], ps[7][:, 400:408].rearrange("p (t h) -> p t h", t=T),
                                          ALU.add).then_inc(s_m, 1)
                    if k == 6:
                        dve.wait_ge(s_gb, l + 1)
                        dve.wait_ge(s_cv, 4 * CK * (l + 1))
                        for h in range(NH):
                            g = ps[4 + h // 2][:, (h % 2) * SEQ:(h % 2 + 1) * SEQ]
                            dve.scalar_tensor_tensor(out=E[:, h // 2, h % 2, 0:SEQ], in0=g, scalar=aa[:, 0, h:h + 1],
                                                     in1=MM[:, :], op0=ALU.add, op1=ALU.min).then_inc(s_e0, 1)
                            dve.scalar_tensor_tensor(out=E[:, h // 2, h % 2, SEQ:], in0=g[:, P:], scalar=aa[:, 1, h:h + 1],
                                                     in1=MM[:, 0:P], op0=ALU.add, op1=ALU.min).then_inc(s_e0, 1)
                    if 8 <= k < 11:
                        attn_max(l, k - 8)
                    if 1 <= k <= LEVELS:
                        level_copy(l, k - 1)
                    if k == 2:
                        convolve(l)
                    if 8 <= k < 11:
                        attn_weights(l, k - 8)
                dve.wait_ge(s_e, l + 1)
                for r, b0, v in ((0, 2, slice(0, SEQ)), (1, 4, slice(SEQ, SEQ + P))):
                    dve.wait_ge(s_qk, 2 * l + r + 1)
                    n = v.stop - v.start
                    for q in range(2):
                        dve.scalar_tensor_tensor(out=E[:, :, q, v], in0=ps[b0 + q][:, 0:2 * n].rearrange("p (c t) -> p c t", c=2),
                                                 scalar=SCALE, in1=E[:, :, q, v], op0=ALU.mult, op1=ALU.mult).then_inc(s_w, 1)
                for t in range(T):
                    dve.wait_ge(s_dn, T * l + t + 1)
                    dve.wait_ge(s_em, l + 1)
                    dve.tensor_tensor(dn[:, 1, t, :], dn[:, 0, t, :], em[:, t, :], ALU.max).then_inc(s_dr, 1)
                    dve.wait_ge(s_dr, 4 * l + 2 * t + 1)
                    dve.reciprocal(dn[:, 1, t, :], dn[:, 1, t, :]).then_inc(s_dr, 1)
                    dve.wait_ge(s_dr, 4 * l + 2 * t + 2)
                    dve.tensor_tensor(OM[:, t, NH:, :], ps[1 + t][:, 0:NH * 65].rearrange("p (h e) -> p h e", h=NH)[:, :, 0:DH],
                                      bc(dn[:, 1, t, :].unsqueeze(2), [P, NH, DH]), ALU.mult).then_inc(s_oh, 1)
                for t in range(T):
                    dve.wait_ge(s_sq, T * l + t + 1)
                    dve.tensor_reduce(hs[:, 0, t, :], SQ[:, t, :, :], AX.X, ALU.add).then_inc(s_hs, 1)
                for t in range(T):
                    dve.wait_ge(s_hr, T * l + t + 1)
                    dve.wait_ge(s_oh, T * (l + 1))
                    dve.tensor_tensor(OM[:, t, :, :], OM[:, t, :, :], bc(hs[:, 1, t, :].unsqueeze(2), [P, 2 * NH, DH]),
                                      ALU.mult).then_inc(s_on, 1)
                    dve.wait_ge(s_on, T * l + t + 1)
                    dve.wait_ge(s_g2, 2 * l + 2)
                    dve.tensor_tensor(OM[:, t, :, :], OM[:, t, :, :], G2[:, t, :, :], ALU.mult).then_inc(s_og, 1)
                dve.wait_ge(s_mt, T * l + 2)
                dve.tensor_copy(mixT[:, 0:4, P:SEQ], ps[0][:, :].rearrange("p (c t) -> p c t", c=4)).then_inc(s_me1, 1)
                add_residual(lambda n, t: dve.wait_ge(s_wo, 4 * l + 2 * n + t + 1))

                normalise(2 * l + 1)
                turned(2 * l + 1, PCf[:, l, :])
                if l == 0:
                    for i in range(DFF // P):
                        dve.wait_ge(s_sg, i + 1)
                        if i >= 4:
                            dve.wait_ge(s_dd, i - 3)
                        dve.tensor_tensor(HT[i % 4], SG[i % 4], ps[i % 4][:, SEQ:2 * SEQ], ALU.mult).then_inc(s_ht, 1)
                    add_residual(lambda n, t: dve.wait_ge(s_dd, DFF // P))

            step = [0]

            def then(ins):
                ins.then_inc(s_rt, 1)
                step[0] += 1
                dve.wait_ge(s_rt, step[0])

            def row(r):
                return RT[:, r, :].rearrange("p (t e) -> p t e", t=T)

            def top(src, eq, cs, first, v):
                then(dve.tensor_reduce(v, row(src), AX.X, ALU.max))
                then(dve.tensor_tensor(row(eq), row(src), bc(v.unsqueeze(2), [P, T, NE]), ALU.is_equal))
                for t in range(T):
                    then(dve.tensor_tensor_scan(row(cs)[:, t, :], row(eq)[:, t, :], MM[:, P:P + NE], 0.0, ALU.add, ALU.add))
                then(dve.scalar_tensor_tensor(out=row(first), in0=row(cs), scalar=1.0, in1=row(eq),
                                              op0=ALU.is_equal, op1=ALU.mult))

            dve.wait_ge(s_lg, 1)
            then(dve.tensor_copy(RT[:, 0, :], ps[7][:, 0:16]))
            top(0, 1, 2, 3, RV[:, 0, :])
            then(dve.scalar_tensor_tensor(out=RT[:, 4, :], in0=RT[:, 3, :], scalar=-BIG, in1=RT[:, 0, :],
                                          op0=ALU.mult, op1=ALU.add))
            top(4, 5, 6, 7, RV[:, 1, :])
            then(dve.tensor_tensor(RT[:, 10, :], RT[:, 3, :], RT[:, 7, :], ALU.add))
            assert step[0] == RT_CHOSEN
            then(dve.tensor_tensor(RV[:, 2, :], RV[:, 1, :], RV[:, 0, :], ALU.subtract))
            assert step[0] == RT_DIFF
            dve.wait_ge(s_rx, 1)
            then(dve.tensor_scalar(RV[:, 4, :], RV[:, 3, :], 1.0, None, ALU.add))
            then(dve.reciprocal(RV[:, 5, :], RV[:, 4, :]))
            then(dve.tensor_tensor(RV[:, 6, :], RV[:, 3, :], RV[:, 5, :], ALU.mult))
            then(dve.tensor_tensor(row(8), row(3), bc(RV[:, 5, :].unsqueeze(2), [P, T, NE]), ALU.mult))
            then(dve.tensor_tensor(row(9), row(7), bc(RV[:, 6, :].unsqueeze(2), [P, T, NE]), ALU.mult))
            then(dve.tensor_tensor(RT[:, 8, :], RT[:, 8, :], RT[:, 9, :], ALU.add))
            dve.wait_ge(s_rk, 1)
            rank = ps[7][:, 32:48].rearrange("p (t e) -> p t e", t=T)
            slots = RC[:, 0, :, :].rearrange("p t (e b) -> p t e b", b=2)
            gates = RC[:, 1, :, :].rearrange("p t (e b) -> p t e b", b=2)
            active = JB[:, 0, :].rearrange("p (e b) -> p e b", b=2)
            for b in range(2):
                then(dve.scalar_tensor_tensor(out=slots[:, :, :, b], in0=rank, scalar=-float(P * b), in1=row(10),
                                              op0=ALU.add, op1=ALU.mult))
                then(dve.tensor_copy(gates[:, :, :, b], row(8)))
                then(dve.tensor_scalar(active[:, :, b], ps[7][:, 48:56], float(P * b), None, ALU.is_gt))
            then(dve.tensor_scalar(RC[:, 0, :, :], RC[:, 0, :, :], -1.0, None, ALU.add))
            then(dve.memset(JB[:, 0, 0:1], 1.0))
            then(dve.tensor_tensor_scan(JB[:, 1, :], JB[:, 0, :], MM[:, P:P + 16], 0.0, ALU.add, ALU.add))
            oh = [OH[:, i, :].rearrange("p (j c) -> p j c", c=16) for i in range(2)]
            full = [P, 16, 16]
            then(dve.tensor_tensor(oh[0], bc(JB[:, 1, :].unsqueeze(1), full), bc(cidx[:, 0, :].unsqueeze(2), full), ALU.is_equal))
            then(dve.tensor_tensor(oh[0], oh[0], bc(JB[:, 0, :].unsqueeze(1), full), ALU.mult))

            def by_job(dst, src):
                then(dve.tensor_tensor(oh[1], oh[0], bc(src.unsqueeze(1), full), ALU.mult))
                then(dve.tensor_reduce(dst, oh[1], AX.X, ALU.add))

            by_job(JB[:, 2, :], cidx[:, 1, :])
            then(dve.tensor_copy(jobs[:, 0:16], JB[:, 2, :]))
            dve.tensor_copy(jobs[:, 16:17], JB[:, 1, 15:16]).then_inc(s_jl, 1)
            for q in range(2):
                for t in range(T):
                    by_job(RC[:, 2 + q, t, :], RC[:, q, t, :])
            dve.wait_ge(s_jl, 1)
            njobs = dve.value_load(jobs[0:1, 16:17], min_val=2, max_val=NCAND)
            NCH = len(ECH)
            with dve.Fori(0, njobs) as j:
                for t in range(T):
                    slot_of = RC[:, 2, t, bass.ds(j, 1)]
                    gate_of = RC[:, 3, t, bass.ds(j, 1)]
                    dve.tensor_scalar(selS[:, t, :], iota[:, :], slot_of, None, ALU.is_equal)
                    ins = dve.tensor_scalar(selG[:, t, :], iota[:, :], slot_of, gate_of, ALU.is_equal, ALU.mult)
                ins.then_inc(s_sel, 1)
                for b in range(2):
                    dve.wait_ge(s_gx, 2 * j + b + 1)
                    dve.tensor_tensor(xeT[:, 4 * b:4 * b + 4, :], ps[6 + b][:, :].rearrange("p (c s) -> p c s", c=4),
                                      bc(PCf[:, 1, 4 * b:4 * b + 4].unsqueeze(2), [P, 4, P]), ALU.mult).then_inc(s_xe, 1)
                for c in range(NCH):
                    dve.wait_ge(s_es, j * NCH + c + 1)
                    dve.wait_ge(s_eu, j * NCH + c + 1)
                    if c >= 2:
                        dve.wait_ge(s_et, j * NCH + c - 1)
                    dve.tensor_tensor(hid[c % 2], sil[c % 2], ps[2 * (c % 2) + 1][:, :], ALU.mult).then_inc(s_eh, 1)
                for n in range(2):
                    for t in range(T):
                        dve.wait_ge(s_cz, 4 * j + 2 * n + t + 1)
                        xs = X[:, t, n * BANK:(n + 1) * BANK]
                        dve.tensor_tensor(xs, xs, ps[2 * n + t][:, :], ALU.add).then_inc(s_ca, 1)
            dve.memset(RV[:, 7, :], 0.0).then_inc(s_fr, 1)

            normalise(2 * DEPTH)
            dve.wait_ge(s_fg, 16)
            for t in range(T):
                dve.wait_ge(s_xn, 2 * (2 * DEPTH) + t + 1)
                dve.tensor_tensor(XN[:, t, :], XN[:, t, :], fgain, ALU.mult).then_inc(s_fin, 1)

        @block.tensor
        def _(pe):
            def turn(i):
                for b in range(4):
                    t, c0 = b // 2, 4 * (b % 2)
                    pe.wait_ge(s_xn, 2 * i + t + 1)
                    for c in range(4):
                        ins = pe.transpose(ps[b][:, c * P:(c + 1) * P], XN[:, t, (c0 + c) * P:(c0 + c + 1) * P], ident[:, :])
                    ins.then_inc(s_xt, 1)

            def wslot(s, k, n):
                return ring[:, s * SLOT:s * SLOT + k * n].rearrange("p (k n) -> p k n", k=k)

            def unit(u, k, n):
                pe.wait_ge(w_loaded[u % RING], LOADED * (u // RING + 1))
                return wslot(u % RING, k, n)

            def project(l, i):
                s = i // 2
                w = unit(unit_base[l] + s, KD, BANK)
                if i >= 2:
                    pe.wait_ge(s_pe, NHALF * l + i - 1)
                b = ps[i % 2]
                if FEATURE_MAJOR[s]:
                    for f in range(2):
                        c0 = (2 * (i % 2) + f) * P
                        for k in range(KD):
                            ins = pe.matmul(b[:, f * SEQ:(f + 1) * SEQ], w[:, k, c0:c0 + P], hT[:, k, :],
                                            start=(k == 0), stop=(k == KD - 1))
                else:
                    t = i % 2
                    for k in range(KD):
                        ins = pe.matmul(b[:, :], hT[:, k, t * P:(t + 1) * P], w[:, k, :], start=(k == 0), stop=(k == KD - 1))
                ins.then_inc(s_pp, 1)

            def level(l, k):
                if k == 0:
                    pe.wait_ge(s_hk, l + 1)
                    q, kk = HQ[:, :], HK[:, :]
                    if l:
                        pe.wait_ge(s_res, 8)
                else:
                    pe.wait_ge(s_qd, (LEVELS - 1) * l + k)
                    pe.wait_ge(s_kd, (LEVELS - 1) * l + k)
                    pe.wait_ge(s_lc, LEVELS * l + k)
                    q, kk = QD[:, k % 2, :], KDk[:, k % 2, :]
                for c in range(2):
                    for p in range(2):
                        r = slice(DH * p, DH * p + DH)
                        if k < 8:
                            for t in range(T):
                                v = slice(c * SEQ + t * P, c * SEQ + (t + 1) * P)
                                ins = pe.matmul(ps[2 + p][:, (2 * c + t) * P:(2 * c + t + 1) * P], kk[r, v], q[r, v],
                                                start=True, stop=True)
                        else:
                            ins = pe.matmul(ps[2 + p][:, c * P:(c + 1) * P], kk[r, c * SEQ:c * SEQ + P],
                                            q[r, c * SEQ + P:(c + 1) * SEQ], start=True, stop=True)
                ins.then_inc(s_lp, 1)

            def attn_scores(l, g):
                if g == 0:
                    pe.wait_ge(s_e0, 8 * (l + 1))
                    pe.wait_ge(s_pe, NHALF * l + 8)
                    pe.wait_ge(s_ls, 2 * l + 2)
                else:
                    pe.wait_ge(s_ex, 3 * l + g)
                heads = range(NFH) if g == 0 else range(4 * (g - 1), 4 * g)
                w, qt = (P, 0) if g == 0 else (SEQ, 1)
                for h in heads:
                    p, c = h % 2, h // 2
                    r = slice(DH * p, DH * p + DH)
                    o = ps[4 + p][:, (c * w) % BANK:(c * w) % BANK + w]
                    nlf = GA[:, 2, :, 2 * NH + h:2 * NH + h + 1]
                    pe.matmul(o, FQ[r, c, qt * P:(qt + 1) * P], FK[r, c, 0:w], start=True, stop=False)
                    if g:
                        pe.matmul(o[:, P:], nlf[:, 1, :].to_broadcast([P, P]), UO[:, 0:P], start=False, stop=False,
                                  skip_group_check=True)
                    pe.matmul(o[:, w - P:], ident[:, :], NM[:, :], start=False, stop=False, skip_group_check=True)
                    ins = pe.matmul(o, nlf[:, 0, :].to_broadcast([P, P]), UO[:, 0:w], start=False, stop=True)
                ins.then_inc(s_S, 1)

            def attn_turn(l, g):
                pe.wait_ge(s_pn, 3 * l + g + 1)
                for p in range(2):
                    if 2 * g + p:
                        pe.wait_ge(s_te, 6 * l + 2 * g + p)
                    for b in range(4):
                        v = (4 * p + b) * P
                        ins = pe.transpose(ps[6][:, b * P:(b + 1) * P], PP[g % 2][:, v:v + P], ident[:, :])
                    ins.then_inc(s_tp, 1)

            def attn_apply(l, g):
                pe.wait_ge(s_te, 6 * l + 2 * g + 2)
                pe.wait_ge(s_pe, NHALF * l + 10)
                pe.wait_ge(s_em, l + 1)
                if g:
                    pe.wait_ge(s_fo, 3 * l + g)
                heads = range(NFH) if g == 0 else range(4 * (g - 1), 4 * g)
                for h in heads:
                    p, c = h % 2, h // 2 if g == 0 else (h // 2) % 2
                    o = ps[7][DH * p:DH * p + DH, c * P:(c + 1) * P]
                    tiles = 1 if g == 0 else T
                    for t in range(tiles):
                        b = 4 * p + (c if g == 0 else 2 * c + t)
                        ins = pe.matmul(o, FV[:, t, h * DH:(h + 1) * DH], PT[:, b * P:(b + 1) * P],
                                        start=(t == 0), stop=(t == tiles - 1))
                ins.then_inc(s_pv, 1)

            pe.wait_ge(s_cst, NCONST)
            pe.wait_ge(s_par, NPAR)
            pe.transpose(ps[6][:, 0:68], PR[:, :], ident[0:68, 0:68]).then_inc(s_prT, 1)

            for l in range(DEPTH):
                turn(2 * l)
                pe.wait_ge(s_hT, 4 * (2 * l) + 4)
                for t in range(T):
                    for k in range(KD):
                        ins = pe.matmul(ps[7][:, t * 16:(t + 1) * 16], hT[:, k, t * P:(t + 1) * P], WG[:, l, k, :],
                                        start=(k == 0), stop=(k == KD - 1))
                ins.then_inc(s_gp, 1)
                project(l, 0)
                project(l, 1)
                pe.wait_ge(s_ls, 2 * l + 1)
                pe.matmul(ps[7][:, 32:36], UO[:, 0:P], GA[:, 1, 0, NH:2 * NH], start=True, stop=True)
                pe.matmul(ps[7][:, 36:40], UO[:, P:2 * P], GA[:, 1, 0, NH:2 * NH], start=True, stop=False)
                pe.matmul(ps[7][:, 36:40], UO[:, 0:P], GA[:, 1, 1, NH:2 * NH], start=False, stop=True).then_inc(s_cb, 1)
                for k in range(STEPS):
                    project(l, k + 2)
                    if k == 0:
                        pe.wait_ge(s_a, 2 * l + 2)
                        for t in range(T):
                            ins = pe.transpose(ps[7][0:NH, 64 + t * P:64 + (t + 1) * P], aa[:, t, :], ident[:, :])
                        ins.then_inc(s_aT, 1)
                    if k == 2:
                        pe.wait_ge(s_g, T * (l + 1))
                        for t in range(T):
                            ins = pe.transpose(ps[7][:, 400 + t * NH:400 + (t + 1) * NH], gT[:, t * P:(t + 1) * P], ident[0:NH, 0:NH])
                        ins.then_inc(s_gi, 1)
                        for h in range(NH):
                            ins = pe.matmul(ps[4 + h // 2][:, (h % 2) * SEQ:(h % 2 + 1) * SEQ], SEL[:, h, :], gT[:, :],
                                            start=True, stop=True)
                        ins.then_inc(s_gb, 1)
                    if k < LEVELS:
                        level(l, k)
                    if k >= 9:
                        attn_apply(l, k - 9)
                    if 7 <= k < 10:
                        attn_scores(l, k - 7) if k == 7 else None
                    if 8 <= k < 11:
                        attn_turn(l, k - 8)
                    if 8 <= k < 10:
                        attn_scores(l, k - 7)
                    if k == 10:
                        pe.wait_ge(s_mc, l + 1)
                        pe.wait_ge(s_lc, LEVELS * (l + 1))
                        for h in range(NH):
                            c, p = h // 2, h % 2
                            r = slice(DH * p, DH * p + DH)
                            ins = pe.matmul(ps[2 + p][:, c * SEQ:(c + 1) * SEQ], MC[r, 2 + c, 0:P], MC[r, c, :],
                                            start=True, stop=True)
                        ins.then_inc(s_qk, 1)
                pe.wait_ge(s_ex, 3 * (l + 1))
                for h in range(NH):
                    c, p = h // 2, h % 2
                    r = slice(DH * p, DH * p + DH)
                    ins = pe.matmul(ps[4 + p][:, c * P:(c + 1) * P], MC[r, 2 + c, P:SEQ], MC[r, c, P:SEQ], start=True, stop=True)
                ins.then_inc(s_qk, 1)
                pe.wait_ge(s_pe, NHALF * (l + 1))
                for h in range(NH):
                    c, p = h // 2, h % 2
                    v = slice(h * DH, (h + 1) * DH)
                    pe.matmul(ps[0][:, h * DH:(h + 1) * DH], SC[:, p, 2 * c, :], HV[:, 0, v], start=True, stop=True)
                    o = ps[0][:, HW + h * DH:HW + (h + 1) * DH]
                    pe.matmul(o, SX[:, p, c, :], HV[:, 0, v], start=True, stop=False)
                    ins = pe.matmul(o, SC[:, p, 2 * c + 1, :], HV[:, 1, v], start=False, stop=True)
                ins.then_inc(s_ho, 1)
                pe.wait_ge(s_w, 4 * (l + 1))
                for t in range(T):
                    for h in range(NH):
                        e = E[:, h // 2, h % 2, :]
                        o = ps[1 + t][:, h * (DH + 1):(h + 1) * (DH + 1)]
                        ins = pe.matmul(o, e[:, t * P:(t + 1) * P], VM[:, 0, h, :], start=True, stop=(t == 0))
                        if t:
                            ins = pe.matmul(o, e[:, SEQ:SEQ + P], VM[:, 1, h, :], start=False, stop=True)
                    ins.then_inc(s_num, 1)
                pe.wait_ge(s_fo, 3 * (l + 1))
                wo = [unit(unit_base[l] + len(SLABS) + n, KD, BANK) for n in range(2)]
                for n in range(2):
                    for t in range(T):
                        for k in range(4, 8):
                            pe.matmul(ps[4 + 2 * n + t][:, :], mixT[:, k, t * P:(t + 1) * P], wo[n][:, k, :],
                                      start=(k == 4), stop=False)
                for t in range(T):
                    pe.wait_ge(s_og, T * l + t + 1)
                    b = ps[3] if t == 0 else ps[0]
                    om = OM[:, t, :, :].rearrange("p h d -> p (h d)")
                    for c in range(4):
                        ins = pe.transpose(b[:, c * P:(c + 1) * P], om[:, c * P:(c + 1) * P], ident[:, :])
                    ins.then_inc(s_mt, 1)
                for n in range(2):
                    for t in range(T):
                        pe.wait_ge(s_me if t == 0 else s_me1, l + 1)
                        for k in range(4):
                            ins = pe.matmul(ps[4 + 2 * n + t][:, :], mixT[:, k, t * P:(t + 1) * P], wo[n][:, k, :],
                                            start=False, stop=(k == 3))
                        ins.then_inc(s_wo, 1)

                turn(2 * l + 1)
                pe.wait_ge(s_hT, 4 * (2 * l + 1) + 4)
                if l == 0:
                    NB = DFF // P
                    ub = len(SLABS) + 2

                    def down(i):
                        c, b = i // 4, i % 4
                        n0 = DCH[c][1]
                        w = unit(ub + 3 * c + 2, n0 // P, D)
                        pe.wait_ge(s_ht, i + 1)
                        for n in range(2):
                            for t in range(T):
                                ins = pe.matmul(ps[4 + 2 * n + t][:, :], HT[i % 4][:, t * P:(t + 1) * P],
                                                w[:, b, n * BANK:(n + 1) * BANK], start=(i == 0), stop=(i == NB - 1))
                        ins.then_inc(s_dd, 1)

                    for i in range(NB):
                        c, b = i // 4, i % 4
                        if i >= 4:
                            pe.wait_ge(s_ht, i - 3)
                        for r in range(2):
                            w = unit(ub + 3 * c + r, KD, DCH[c][1])
                            for k in range(KD):
                                ins = pe.matmul(ps[i % 4][:, r * SEQ:(r + 1) * SEQ], w[:, k, b * P:(b + 1) * P], hT[:, k, :],
                                                start=(k == 0), stop=(k == KD - 1))
                        ins.then_inc(s_gu, 1)
                        if i >= 2:
                            down(i - 2)
                    down(NB - 2)
                    down(NB - 1)

            for t in range(T):
                for k in range(KD):
                    ins = pe.matmul(ps[7][:, t * NE:(t + 1) * NE], hT[:, k, t * P:(t + 1) * P], RW[:, k, :],
                                    start=(k == 0), stop=(k == KD - 1))
            ins.then_inc(s_lg, 1)
            pe.wait_ge(s_rt, RT_CHOSEN)
            m = [RT[:, 10, t * NE:(t + 1) * NE] for t in range(T)]
            pe.matmul(ps[7][:, 32:40], UO[:, 0:P], m[0], start=True, stop=True)
            pe.matmul(ps[7][:, 40:48], UO[:, P:], m[0], start=True, stop=False)
            pe.matmul(ps[7][:, 40:48], UO[:, 0:P], m[1], start=False, stop=True)
            pe.matmul(ps[7][:, 48:56], UO[:, P:], m[0], start=True, stop=False)
            pe.matmul(ps[7][:, 48:56], UO[:, P:], m[1], start=False, stop=True).then_inc(s_rk, 1)

            pe.wait_ge(s_jl, 1)
            njobs = pe.value_load(jobs[0:1, 16:17], min_val=2, max_val=NCAND)
            NCH = len(ECH)
            with pe.Fori(0, njobs) as j:
                def expert_unit(i, k, n):
                    s = i % ERING
                    pe.wait_ge(w_loaded[s], j * (PER_JOB * LOADED) + LOADED * (uses_before[s] + i // ERING + 1))
                    return wslot(s, k, n)

                def turn_hidden(c):
                    pe.wait_ge(s_eh, j * NCH + c + 1)
                    if c:
                        pe.wait_ge(s_ec, j * NCH + c)
                    for b in range(4):
                        ins = pe.transpose(ps[6][:, b * P:(b + 1) * P], hid[c % 2][:, b * P:(b + 1) * P], ident[:, :])
                    ins.then_inc(s_et, 1)

                def expert_down(c):
                    w = expert_unit(3 * c + 2, 4, D)
                    pe.wait_ge(s_ec, j * NCH + c + 1)
                    for b in range(4):
                        for n in range(2):
                            ins = pe.matmul(ps[4 + n][:, :], hidT[c % 2][:, b * P:(b + 1) * P], w[:, b, n * BANK:(n + 1) * BANK],
                                            start=(c == 0 and b == 0), stop=(c == NCH - 1 and b == 3))
                    ins.then_inc(s_ed, 1)

                pe.wait_ge(s_sel, j + 1)
                for b in range(2):
                    for c in range(4):
                        for t in range(T):
                            ins = pe.matmul(ps[6 + b][:, c * P:(c + 1) * P], XN[:, t, (4 * b + c) * P:(4 * b + c + 1) * P],
                                            selS[:, t, :], start=(t == 0), stop=(t == T - 1))
                    ins.then_inc(s_gx, 1)
                for t in range(T):
                    ins = pe.transpose(ps[4][:, t * P:(t + 1) * P], selG[:, t, :], ident[:, :])
                ins.then_inc(s_sgT, 1)
                pe.wait_ge(s_xe, 2 * j + 2)
                for c in range(NCH):
                    for r in range(2):
                        w = expert_unit(3 * c + r, KD, BANK)
                        if r == 0 and c >= 2:
                            pe.wait_ge(s_eh, j * NCH + c - 1)
                        for k in range(KD):
                            ins = pe.matmul(ps[2 * (c % 2) + r][:, :], xeT[:, k, :], w[:, k, :],
                                            start=(k == 0), stop=(k == KD - 1))
                        ins.then_inc((s_eg, s_eu)[r], 1)
                        if c:
                            if r == 0:
                                turn_hidden(c - 1)
                            else:
                                if c == 1:
                                    pe.wait_ge(s_sgc, j + 1)
                                expert_down(c - 1)
                turn_hidden(NCH - 1)
                expert_down(NCH - 1)
                for n in range(2):
                    pe.wait_ge(s_ey, 2 * j + n + 1)
                    for t in range(T):
                        pe.matmul(ps[2 * n + t][:, :], selGT[:, t * P:(t + 1) * P], ye[:, n * BANK:(n + 1) * BANK],
                                  start=True, stop=True).then_inc(s_cz, 1)


_INS = ['x', 'attn_norm', 'w_in', 'hgrn_lb', 'hgrn_norm', 'mlstm_conv', 'mlstm_b_i', 'mlstm_b_f', 'mlstm_norm',
        'fox_b_f', 'w_out', 'ffn_norm', 'dense_w_gate', 'dense_w_up', 'dense_w_down', 'router', 'moe_w_gate',
        'moe_w_up', 'moe_w_down', 'final_norm']


def kernel(**inputs):
    import numpy as _np
    import concourse.bacc as _bacc
    from concourse import mybir as _mybir
    from concourse.bass_utils import run_bass_kernel_spmd as _run

    nc = _bacc.Bacc("TRN2", target_bir_lowering=False, num_devices=1)
    arrays, args = {}, []
    for name in _INS:
        a = _np.ascontiguousarray(inputs[name])
        arrays[f"in_{name}_dram"] = a
        args.append(nc.dram_tensor(f"in_{name}_dram", a.shape, _mybir.dt.from_np(a.dtype), kind="ExternalInput").ap())
    shape = _np.shape(inputs['x'])
    args.append(nc.dram_tensor("out_0_dram", shape, _mybir.dt.from_np(_np.dtype('float32')), kind="ExternalOutput").ap())
    bass_hybrid_trunk_kernel(nc, *args)
    r = _run(nc, [arrays], core_ids=[0])
    return r.results[0]["out_0_dram"]
```

```python
from contextlib import ExitStack

import concourse.bass as bass
from concourse import mybir

P = 128
F32 = mybir.dt.float32
F32R = mybir.dt.float32r
I32 = mybir.dt.int32
ALU = mybir.AluOpType
ACT = mybir.ActivationFunctionType
AX = mybir.AxisListType

EPS = 1e-6
BIG = 1e30
BANK = 512


def bass_hybrid_trunk_kernel(nc, x, attn_norm, w_in, hgrn_lb, hgrn_norm, mlstm_conv, mlstm_b_i,
                             mlstm_b_f, mlstm_norm, fox_b_f, w_out, ffn_norm, dense_w_gate,
                             dense_w_up, dense_w_down, router, moe_w_gate, moe_w_up, moe_w_down,
                             final_norm, out):
    _, SEQ, D = x.shape
    DEPTH = w_in.shape[0]
    T = SEQ // P
    KD = D // P
    HW = hgrn_norm.shape[1]
    FW = D - 2 * HW
    DH = 64
    NH = HW // DH
    NFH = FW // DH
    CK = mlstm_conv.shape[1]
    DFF = dense_w_gate.shape[2]
    NB = DFF // P
    NE = router.shape[2]
    FE = moe_w_gate.shape[3]
    assert (T, KD, HW, FW, DEPTH, NE, CK) == (2, 8, 256, 512, 2, 8, 4)
    SCALE = DH ** -0.5

    HQ0, HF0, HI0, HG0 = 0, HW, 2 * HW, 3 * HW
    MQ0 = 4 * HW
    MV0 = MQ0 + 2 * HW
    MI0 = MV0 + HW
    MO0 = MI0 + 2 * NH
    FQ0 = MO0 + HW
    FK0, FV0, FF0 = FQ0 + FW, FQ0 + 2 * FW, FQ0 + 3 * FW
    SLABS = [[(HF0, HW), (HQ0, HW)], [(MQ0, 2 * HW)], [(FQ0, FW)], [(FK0, FW)], [(FV0, FW)],
             [(MV0, HW), (MO0, HW)], [(HI0, 2 * HW)]]
    FEATURE_MAJOR = [True, True, True, True, False, False, False]
    NHALF = 2 * len(SLABS)
    STEPS = NHALF - 2
    LEVELS = 9

    SLOT = KD * BANK
    RING = 6
    MIX = 3
    DCH = [(c, min(BANK, DFF - c)) for c in range(0, DFF, BANK)]
    ECH = [(c, BANK) for c in range(0, FE, BANK)]
    MIX_UNITS = len(SLABS) + 2
    DENSE0 = MIX_UNITS
    unit_base = [0, MIX_UNITS + 3 * len(DCH)]
    UNITS = 2 * MIX_UNITS + 3 * len(DCH)
    slot_of = [u % MIX for u in range(MIX_UNITS)] + [u % RING for u in range(3 * len(DCH))] + \
        [u % MIX for u in range(MIX_UNITS)]
    turn_of = [slot_of[:u + 1].count(slot_of[u]) for u in range(UNITS)]
    NCH = len(ECH)
    ORDER = []
    for c in range(NCH):
        ORDER += [("gate", c, 0), ("gate", c, 1), ("up", c, 0), ("up", c, 1)]
        if c:
            ORDER += [("down", c - 1, 0), ("down", c - 1, 1)]
    ORDER += [("down", NCH - 1, 0), ("down", NCH - 1, 1)]
    AT = {piece: q for q, piece in enumerate(ORDER)}
    NPC = len(ORDER)
    PIECE = SLOT // 2
    RAW = 7
    SPLIT = 3
    assert NPC % RAW == 0 and NPC % SPLIT == 0
    LOADED = 32
    SHARED = 42240
    MAXJOBS = NE + 2 * SEQ // (P + 1)

    with ExitStack() as ctx:
        def sb(name, shape, dt=F32):
            return ctx.enter_context(nc.sbuf_tensor(name, shape, dt))

        def sem(name):
            return ctx.enter_context(nc.semaphore(name))

        ps = [ctx.enter_context(nc.psum_tensor(f"bank{i}", [P, BANK], F32)) for i in range(8)]

        X = sb("X", [P, T, D])
        XN = sb("XN", [P, T, D])
        hT = sb("hT", [P, KD, SEQ])
        shared = -(-nc.sbuf_base // 32) * 32
        sb("arena", [P, SHARED])
        taken = {"layers": 0, "experts": 0}

        def phase(which, name, shape, dt=F32):
            at = taken[which]
            n = 1
            for d in shape[1:]:
                n *= d
            taken[which] = at + (n + 7) // 8 * 8
            assert taken[which] <= SHARED, (which, name)
            return nc.alloc_sbuf_tensor_at(name, shape, dt, offset=shared + 4 * at)

        ring = phase("layers", "ring", [P, MIX * SLOT])
        winh = phase("layers", "winh", [P, 2, KD, SEQ], F32R)
        winl = phase("layers", "winl", [P, 2, KD, SEQ], F32R)
        hTh = phase("layers", "hTh", [P, KD, SEQ], F32R)
        hTl = phase("layers", "hTl", [P, KD, SEQ], F32R)
        assert taken["layers"] == RING * SLOT
        last_slot = phase("layers", "attention", [P, 4096])
        FQ = last_slot[:, 0:1024].rearrange("p (c t) -> p c t", c=4)
        FK = last_slot[:, 1024:2048].rearrange("p (c t) -> p c t", c=4)
        FV = last_slot[:, 2048:3072].rearrange("p (t n) -> p t n", t=T)
        PT = last_slot[:, 3072:4096]
        OM = last_slot[:, 0:1024].rearrange("p (t h d) -> p t h d", t=T, h=2 * NH)
        SQ = last_slot[:, 1024:2048].rearrange("p (t h d) -> p t h d", t=T, h=2 * NH)
        XNf = XN[:, :, :].rearrange("p t d -> p (t d)")
        FZ, TMP, LS, NK = (XNf[:, i * 512:(i + 1) * 512] for i in range(4))
        PP = [XNf[:, g * 1024:(g + 1) * 1024] for g in range(2)]
        HQ = phase("layers", "HQ", [P, 512])
        HK = phase("layers", "HK", [P, 512])
        LF = phase("layers", "LF", [P, 512])
        B = phase("layers", "B", [P, 512])
        DX = phase("layers", "DX", [P, 2, 512])
        QD = phase("layers", "QD", [P, 2, 512])
        KDk = phase("layers", "KDk", [P, 2, 512])
        SC = phase("layers", "SC", [P, 2, 4, P])
        SX = phase("layers", "SX", [P, 2, 2, P])
        HV = phase("layers", "HV", [P, T, HW])
        MC = phase("layers", "MC", [P, 4, SEQ])
        ER = phase("layers", "ER", [P, NH * 384])
        MR = ER[:, 0:4 * (SEQ + 3)].rearrange("p (c t) -> p c t", c=4)
        E = ER[:, :].rearrange("p (c q n) -> p c q n", c=2, q=2)
        VM = phase("layers", "VM", [P, T, NH, DH + 1])
        G2 = phase("layers", "G2", [P, T, 2 * NH, DH])
        mixT = phase("layers", "mixT", [P, KD, SEQ])

        ident = sb("ident", [P, P])
        UO = sb("UO", [P, 2 * P])
        NM = sb("NM", [P, P])
        MM = sb("MM", [P, 2 * P])
        LM = sb("LM", [P, 8, P])
        SEL = sb("SEL", [NH, NH, P])
        mhalf = sb("mhalf", [P, 2 * NH])
        PR = sb("PR", [68, P])
        PC = sb("PC", [P, 68])
        GB = sb("GB", [P, DEPTH, 16])
        HNG = sb("HNG", [P, DEPTH, 2 * HW])
        WG = sb("WG", [P, DEPTH, KD, 16])
        RW = sb("RW", [P, KD, NE])
        LB = sb("LB", [P, 5, 2])
        LBT = sb("LBT", [P, 4, 2])
        st = sb("st", [P, 2 * DEPTH + 1, 2, T])
        GA = sb("GA", [P, 4, T, 16])
        aa = sb("aa", [P, T, NH])
        bb = sb("bb", [P, T, NH])
        gT = sb("gT", [NH, SEQ])
        em = sb("em", [P, T, NH])
        nmx = sb("nmx", [P, 3, 8])
        rs = sb("rs", [P, 3, 2, 8])
        dn = sb("dn", [P, 2, T, NH])
        hs = sb("hs", [P, 2, T, 2 * NH])

        PCa = PC[:, 0:16].rearrange("p (l c) -> p l c", l=DEPTH)
        PCf = PC[:, 16:32].rearrange("p (l c) -> p l c", l=DEPTH)
        PCc = PC[:, 32:64].rearrange("p (l j c) -> p l j c", l=DEPTH, j=CK)
        PCl = PC[:, 64:68].rearrange("p (l c) -> p l c", l=DEPTH)

        taken["dense"] = 0
        dring = phase("dense", "dring", [P, RING * SLOT])
        guh = phase("dense", "guh", [P, 2, 2, KD, P], F32R)
        gul = phase("dense", "gul", [P, 2, 2, KD, P], F32R)
        dwh = phase("dense", "dwh", [P, 2, D], F32R)
        dwl = phase("dense", "dwl", [P, 2, D], F32R)
        dTh = phase("dense", "dTh", [P, KD, SEQ], F32R)
        dTl = phase("dense", "dTl", [P, KD, SEQ], F32R)
        HTh = phase("dense", "HTh", [P, 2, SEQ], F32R)
        HTl = phase("dense", "HTl", [P, 2, SEQ], F32R)
        SG = [XNf[:, i * 256:(i + 1) * 256] for i in range(4)]
        HT = [XNf[:, 1024 + i * 256:1280 + i * 256] for i in range(4)]
        raw = phase("experts", "raw", [P, RAW, PIECE])
        high = phase("experts", "high", [P, SPLIT, PIECE], F32R)
        low = phase("experts", "low", [P, SPLIT, PIECE], F32R)
        egain = phase("experts", "egain", [P, D])
        xeh = phase("experts", "xeh", [P, KD, P], F32R)
        xel = phase("experts", "xel", [P, KD, P], F32R)
        sil = phase("experts", "sil", [P, 2, BANK])
        hid = phase("experts", "hid", [P, 2, BANK])
        hdh = phase("experts", "hdh", [P, 2, BANK], F32R)
        hdl = phase("experts", "hdl", [P, 2, BANK], F32R)
        yeh = phase("experts", "yeh", [P, D], F32R)
        yel = phase("experts", "yel", [P, D], F32R)
        selS = phase("experts", "selS", [P, T, P])
        selT = phase("experts", "selT", [P, SEQ], F32R)
        gcol = phase("experts", "gcol", [P, T])
        gslot = phase("experts", "gslot", [P, 1])
        fgain = hT[:, 0:4, :].rearrange("p a b -> p (a b)")
        iota = sb("iota", [P, P])
        cidx = sb("cidx", [P, 2, 16])
        RT = phase("experts", "RT", [P, 12, 16])
        RV = sb("RV", [P, 8, T])
        RC = phase("experts", "RC", [P, 4, T, 16])
        OH = phase("experts", "OH", [P, 2, 256])
        JB = sb("JB", [P, 5, 16])
        jobs = sb("jobs", [P, 32], I32)

        s_x = sem("x_loaded")
        s_rows = sem("gain_rows_loaded")
        s_par = sem("gate_params_loaded")
        s_hg = sem("head_gains_loaded")
        s_rw = sem("router_loaded")
        w_loaded = [sem(f"slot{i}_loaded") for i in range(RING)]
        raw_loaded = [sem(f"raw{i}_loaded") for i in range(RAW)]
        s_fg = sem("final_gain_loaded")
        s_out = sem("out_stored")
        s_cst = sem("consts_ready")
        s_prT = sem("param_rows_turned")
        s_pc = sem("param_cols_ready")
        s_lb = sem("lower_bound_steps")
        s_lba = sem("lower_bound_logs")
        s_ss = sem("square_sums")
        s_rms0 = sem("mean_squares")
        s_rms = sem("inv_rms")
        s_xn = sem("normalised")
        s_xt = sem("normalised_turned")
        s_hT = sem("hT_ready")
        s_res = sem("residual_added")
        s_gp = sem("gates_product")
        s_gv = sem("gate_values")
        s_ga = sem("gate_logs")
        s_ls = sem("gate_logsigmoids")
        s_cb = sem("mlstm_cumsum")
        s_a = sem("mlstm_a")
        s_aT = sem("mlstm_a_turned")
        s_g = sem("mlstm_running_max")
        s_gb = sem("mlstm_g_spread")
        s_m = sem("mlstm_m")
        s_em = sem("mlstm_floor")
        s_e0 = sem("mlstm_exponents")
        s_e = sem("mlstm_decays")
        s_pp = sem("projection_half")
        s_pe = sem("projection_evacuated")
        s_h1 = sem("hgrn_gate_logs")
        s_h2 = sem("hgrn_gate_sums")
        s_hk = sem("hgrn_keys")
        s_b = sem("hgrn_cumulated")
        s_d0 = sem("level_differences")
        s_dxa = sem("level_abs")
        s_dx = sem("level_decays")
        s_qd = sem("level_queries")
        s_kd = sem("level_keys")
        s_lp = sem("level_scores")
        s_lc = sem("level_copied")
        s_pad = sem("conv_padding")
        s_cv = sem("conv_steps")
        s_mc = sem("conv_silu")
        s_S = sem("attn_scores")
        s_mx = sem("attn_max")
        s_nx = sem("attn_neg_max")
        s_ex = sem("attn_exp")
        s_rr = sem("attn_inv_sum")
        s_pn = sem("attn_weights")
        s_tp = sem("attn_turned")
        s_te = sem("attn_turned_copied")
        s_pv = sem("attn_out")
        s_fo = sem("attn_out_copied")
        s_qk = sem("mlstm_scores")
        s_w = sem("mlstm_weights")
        s_ho = sem("hgrn_out")
        s_num = sem("mlstm_sums")
        s_oc = sem("hgrn_out_copied")
        s_dn = sem("mlstm_abs_den")
        s_dr = sem("mlstm_den_steps")
        s_oh = sem("mlstm_out")
        s_sq = sem("head_squares")
        s_hs = sem("head_square_sums")
        s_hr0 = sem("head_mean_squares")
        s_hr = sem("head_inv_rms")
        s_gr = sem("gate_activations")
        s_g2 = sem("gate_gain_steps")
        s_on = sem("heads_normalised")
        s_og = sem("heads_gated")
        s_mt = sem("mix_turned")
        s_me = sem("mix_turned_copied")
        s_wo = sem("out_projection")
        s_gu = sem("dense_gate_up")
        s_sg = sem("dense_silu")
        s_ht = sem("dense_hidden")
        s_dd = sem("dense_down")
        s_hTh = sem("hT_high")
        s_hTl = sem("hT_low")
        s_wih = sem("projection_weights_high")
        s_wil = sem("projection_weights_low")
        s_guh = sem("dense_gate_up_high")
        s_gul = sem("dense_gate_up_low")
        s_dwh = sem("dense_down_high")
        s_dwl = sem("dense_down_low")
        s_hdh = sem("dense_hidden_high")
        s_hdl = sem("dense_hidden_low")
        s_lg = sem("router_logits")
        s_rt = sem("routing_steps")
        s_rx = sem("routing_exp")
        s_rk = sem("routing_ranks")
        s_jl = sem("job_list")
        s_sel = sem("job_selection")
        s_gc = sem("job_gates")
        s_gx = sem("job_gathered")
        s_sT = sem("job_selection_turned")
        s_sTc = sem("job_selection_copied")
        s_eg0 = sem("expert_gain_loaded")
        s_xg = sem("tokens_with_gain")
        s_hi = sem("piece_high")
        s_lo = sem("piece_low")
        s_used = sem("piece_used")
        s_xh = sem("job_tokens_high")
        s_xl = sem("job_tokens_low")
        s_es = sem("expert_silu")
        s_eh = sem("expert_hidden")
        s_et = sem("expert_hidden_turned")
        s_hh = sem("expert_hidden_high")
        s_hl = sem("expert_hidden_low")
        s_yh = sem("expert_out_high")
        s_yl = sem("expert_out_low")
        s_cz = sem("expert_combined")
        s_ca = sem("expert_added")
        s_me1 = sem("mix_turned_copied_tile1")
        s_gi = sem("mlstm_g_turned")
        s_fin = sem("final_scaled")

        def halves(ap, k):
            return ap.rearrange("p (n m) -> p n m", m=2 ** k)

        def nth_piece(j, q):
            return NPC * j + q + 1

        def nth_use(j, q):
            return NPC * j + q + 1 + SPLIT

        def half_columns(u, h):
            w = ring[:, slot_of[u] * SLOT:(slot_of[u] + 1) * SLOT].rearrange("p (k n) -> p k n", k=KD)
            return w[:, :, h * SEQ:(h + 1) * SEQ]

        def block_weights(i):
            c, b = i // 4, i % 4
            n = DCH[c][1]
            views = []
            for r in range(3):
                at = slot_of[DENSE0 + 3 * c + r] * SLOT
                w = dring[:, at:at + KD * n]
                if r < 2:
                    views.append(w.rearrange("p (k n) -> p k n", k=KD)[:, :, b * P:(b + 1) * P])
                else:
                    views.append(w[:, b * D:(b + 1) * D])
            return views

        consts = []
        NPAR = 16 * 5 * DEPTH
        RT_CHOSEN = 13
        RT_DIFF = RT_CHOSEN + 1

        block = ctx.enter_context(nc.Block())

        @block.sync
        def _(sp):
            sp.dma_start(X[:, :, :], x[0].rearrange("(t p) d -> p t d", p=P)).then_inc(s_x, 16)
            sp.dma_start(PR[0:16, :], attn_norm.rearrange("l (c p) -> (l c) p", p=P)).then_inc(s_rows, 16)
            sp.dma_start(PR[16:32, :], ffn_norm.rearrange("l (c p) -> (l c) p", p=P)).then_inc(s_rows, 16)
            sp.dma_start(PR[32:64, :], mlstm_conv.rearrange("l j (c p) -> (l j c) p", p=P)).then_inc(s_rows, 16)
            sp.dma_start(PR[64:68, :], hgrn_lb.rearrange("l (c p) -> (l c) p", p=P)).then_inc(s_rows, 16)
            for l in range(DEPTH):
                for src, c0, n in ((mlstm_b_i, 0, NH), (mlstm_b_f, NH, NH), (fox_b_f, 2 * NH, NFH)):
                    sp.dma_start(GB[:, l, c0:c0 + n], src[l:l + 1, :].to_broadcast([P, n])).then_inc(s_par, 16)
                wi = w_in[l].rearrange("(k p) n -> p k n", p=P)
                sp.dma_start(WG[:, l, :, 0:2 * NH], wi[:, :, MI0:MI0 + 2 * NH]).then_inc(s_par, 16)
                sp.dma_start(WG[:, l, :, 2 * NH:16], wi[:, :, FF0:FF0 + NFH]).then_inc(s_par, 16)

            def slot(u, k, n):
                r = dring if DENSE0 <= u < unit_base[1] else ring
                return r[:, slot_of[u] * SLOT:slot_of[u] * SLOT + k * n].rearrange("p (k n) -> p k n", k=k)

            released = {}

            def claim(u, s):
                before = [v for v in range(u) if slot_of[v] == s]
                if before:
                    sp.wait_ge(*released[before[-1]])
                if s >= MIX and u < unit_base[1] and not before:
                    sp.wait_ge(s_pp, NHALF)
                return s

            def columns(u, w, pieces):
                s, at = claim(u, slot_of[u]), 0
                wr = w.rearrange("(k p) n -> p k n", p=P)
                total = sum(n for _, n in pieces)
                for c0, n in pieces:
                    sp.dma_start(slot(u, KD, total)[:, :, at:at + n], wr[:, :, c0:c0 + n])\
                        .then_inc(w_loaded[s], LOADED // len(pieces))
                    at += n

            def rows(u, w, r0, n):
                s = claim(u, slot_of[u])
                sp.dma_start(slot(u, n // P, D), w[r0:r0 + n, :].rearrange("(j p) n -> p j n", p=P))\
                    .then_inc(w_loaded[s], LOADED)

            for l in range(DEPTH):
                u = unit_base[l]
                for i, pieces in enumerate(SLABS):
                    columns(u + i, w_in[l], pieces)
                    released[u + i] = (s_wil, NHALF * l + 2 * i + 2)
                    if l == 0 and i == 0:
                        for ll in range(DEPTH):
                            sp.dma_start(HNG[:, ll, 0:HW], hgrn_norm[ll:ll + 1, :].to_broadcast([P, HW])).then_inc(s_hg, 16)
                            sp.dma_start(HNG[:, ll, HW:], mlstm_norm[ll:ll + 1, :].to_broadcast([P, HW])).then_inc(s_hg, 16)
                        sp.dma_start(RW[:, :, :], router[0].rearrange("(k p) e -> p k e", p=P)).then_inc(s_rw, 16)
                u += len(SLABS)
                for n in range(2):
                    columns(u + n, w_out[l], [(n * BANK, BANK)])
                    released[u + n] = (s_wo, 4 * l + 2 * n + 2)
                u += 2
                if l == 0:
                    for c0, n in DCH:
                        columns(u, dense_w_gate[0], [(c0, n)])
                        columns(u + 1, dense_w_up[0], [(c0, n)])
                        rows(u + 2, dense_w_down[0], c0, n)
                        blocks = (c0 + n) // P
                        released[u] = released[u + 1] = (s_gul, blocks)
                        released[u + 2] = (s_dwl, blocks)
                        u += 3

            def job(j, e):
                for q, (kind, c, h) in enumerate(ORDER):
                    c0, n = ECH[c]
                    if isinstance(j, int) and q == 4:
                        sp.wait_ge(s_res, 12)
                        sp.dma_start(egain[:, :], ffn_norm[DEPTH - 1:DEPTH, :].to_broadcast([P, D])).then_inc(s_eg0, 16)
                    if q >= RAW or not isinstance(j, int):
                        sp.wait_ge(s_lo, nth_piece(j, q - RAW))
                    else:
                        if q < 2 * MIX:
                            claim(UNITS, q // 2)
                        else:
                            sp.wait_ge(s_pp, NHALF * DEPTH)
                    if kind == "down":
                        m = n // 2
                        src = moe_w_down[0, bass.ds(e, 1), c0 + h * m:c0 + (h + 1) * m, :]
                        k = m // P
                    else:
                        m = D // 2
                        w = moe_w_gate if kind == "gate" else moe_w_up
                        src = w[0, bass.ds(e, 1), h * m:(h + 1) * m, c0:c0 + n]
                        k = m // P
                    sp.dma_start(raw[:, q % RAW, :].rearrange("p (k n) -> p k n", k=k),
                                 src.rearrange("o (k p) n -> p (o k) n", p=P)).then_inc(raw_loaded[q % RAW], 16)

            job(0, 0)
            sp.wait_ge(s_jl, 1)
            njobs = sp.value_load(jobs[0:1, 16:17], min_val=2, max_val=MAXJOBS)
            with sp.Fori(1, njobs) as j:
                e = sp.value_load(jobs[0:1, bass.ds(j, 1)], min_val=0, max_val=NE - 1)
                job(j, e)
            sp.wait_ge(s_lg, 1)
            sp.dma_start(fgain, final_norm.rearrange("(a d) -> a d", a=1).to_broadcast([P, D])).then_inc(s_fg, 16)
            for t in range(T):
                sp.wait_ge(s_fin, t + 1)
                sp.dma_start(out[0, t * P:(t + 1) * P, :], XN[:, t, :]).then_inc(s_out, 16)
            sp.wait_ge(s_out, 16 * T)

        @block.gpsimd
        def _(pool):
            n = [0]

            def done(ins):
                ins.then_inc(s_cst, 1)
                n[0] += 1
                return n[0]

            def select(ap, op, pattern, base, mult, fill):
                pool.wait_ge(s_cst, n[0])
                done(pool.affine_select(out=ap, in_=ap, compare_op=op, fill=fill, base=base,
                                        pattern=pattern, channel_multiplier=mult))

            def inv_rms(i):
                pool.wait_ge(s_ss, 2 * i + 2)
                pool.tensor_scalar(st[:, i, 1, :], st[:, i, 0, :], 1.0 / D, EPS, ALU.mult, ALU.add).then_inc(s_rms0, 1)
                pool.wait_ge(s_rms0, i + 1)
                pool.tensor_tensor(st[:, i, 1, :], st[:, i, 1, :], mhalf[:, 0:T], ALU.pow).then_inc(s_rms, 1)

            done(pool.memset(ident[:, :], 0.0))
            select(ident[:, :], ALU.not_equal, [[-1, P]], 0, 1, 1.0)
            done(pool.memset(mhalf[:, :], -0.5))
            done(pool.memset(UO[:, :], 1.0))
            select(UO[:, 0:P], ALU.is_ge, [[1, P]], 0, -1, 0.0)
            done(pool.memset(NM[:, :], 0.0))
            select(NM[:, :], ALU.is_ge, [[-1, P]], 0, 1, -BIG)
            done(pool.memset(MM[:, :], 0.0))
            select(MM[:, 0:P], ALU.is_ge, [[1, P]], 0, -1, -BIG)
            pool.wait_ge(s_cst, n[0])
            inv_rms(0)
            done(pool.memset(LM[:, :, :], 0.0))
            for k in range(1, 8):
                h = 2 ** (k - 1)
                v = halves(LM[:, k, :], k)[:, :, h:2 * h]
                pool.wait_ge(s_cst, n[0])
                done(pool.memset(v, 1.0))
                select(v, ALU.is_ge, [[-2 * h, P // (2 * h)], [0, h]], 0, 1, 0.0)
                select(v, ALU.is_ge, [[2 * h, P // (2 * h)], [0, h]], h - 1, -1, 0.0)
            pool.wait_ge(s_cst, n[0])
            done(pool.tensor_copy(LM[:, 0, :], ident[:, :]))
            done(pool.memset(SEL[:, :, :], 0.0))
            select(SEL[:, :, :], ALU.not_equal, [[-1, NH], [0, P]], 0, 1, -1.0)
            done(pool.iota(iota[:, :], [[1, P]], base=0, channel_multiplier=0,
                           allow_small_or_imprecise_dtypes=True))
            done(pool.iota(cidx[:, 0, :], [[1, 16]], base=1, channel_multiplier=0,
                           allow_small_or_imprecise_dtypes=True))
            done(pool.iota(cidx[:, 1, :], [[1, NE], [0, 2]], base=0, channel_multiplier=0,
                           allow_small_or_imprecise_dtypes=True))
            nconst = n[0]
            consts.append(nconst)

            for l in range(DEPTH):
                if l:
                    inv_rms(2 * l)
                if l:
                    pool.wait_ge(s_res, 8)
                pool.memset(SC[:, :, :, :], 0.0)
                pool.memset(VM[:, :, :, DH:DH + 1], 1.0)
                pool.memset(MR[:, :, 0:CK - 1], 0.0).then_inc(s_pad, 1)
                for k in range(1, LEVELS):
                    pool.wait_ge(s_dx, (LEVELS - 1) * l + k)
                    pool.wait_ge(s_hk, l + 1)
                    if k >= 3:
                        pool.wait_ge(s_lp, LEVELS * l + k - 1)
                    elif l:
                        pool.wait_ge(s_lp, LEVELS * l)
                    pool.tensor_tensor(KDk[:, k % 2, :], HK[:, :], DX[:, k % 2, :], ALU.mult).then_inc(s_kd, 1)
                pool.wait_ge(s_gr, l + 1)
                pool.tensor_scalar(G2[:, :, NH:, :], G2[:, :, NH:, :], 0.5, 0.5, ALU.mult, ALU.add).then_inc(s_g2, 1)
                pool.wait_ge(s_g2, 2 * l + 1)
                pool.wait_ge(s_hg, 16 * 2 * DEPTH)
                g2 = G2[:, :, :, :].rearrange("p t h d -> p t (h d)")
                pool.tensor_tensor(g2, g2, HNG[:, l, :].unsqueeze(1).to_broadcast([P, T, 2 * HW]), ALU.mult).then_inc(s_g2, 1)
                for t in range(T):
                    pool.wait_ge(s_hs, T * l + t + 1)
                    pool.tensor_scalar(hs[:, 1, t, :], hs[:, 0, t, :], 1.0 / DH, EPS, ALU.mult, ALU.add).then_inc(s_hr0, 1)
                    pool.wait_ge(s_hr0, T * l + t + 1)
                    pool.tensor_tensor(hs[:, 1, t, :], hs[:, 1, t, :], mhalf[:, :], ALU.pow).then_inc(s_hr, 1)
                inv_rms(2 * l + 1)
            pool.wait_ge(s_eg0, 16)
            for t in range(T):
                pool.wait_ge(s_xt, 4 * (2 * DEPTH - 1) + 2 * t + 2)
                pool.tensor_tensor(XN[:, t, :], XN[:, t, :], egain[:, :], ALU.mult).then_inc(s_xg, 1)
            inv_rms(2 * DEPTH)

        NCONST = consts[0]

        @block.scalar
        def _(act):
            def square_sums(i, njobs=None):
                if i == 0:
                    act.wait_ge(s_x, 16)
                elif i < 2 * DEPTH:
                    act.wait_ge(s_res, 4 * i)
                for t in range(T):
                    if i == 2 * DEPTH:
                        act.wait_ge(s_ca, 4 * njobs + 2 * t + 2)
                    act.activation(XN[:, t, :], X[:, t, :], ACT.Square, accum_out=st[:, i, 0, t:t + 1]).then_inc(s_ss, 1)

            def evacuate(l, i):
                act.wait_ge(s_pp, NHALF * l + i + 1)
                b = ps[i % 2]
                two = b[:, :].rearrange("p (c t) -> p c t", c=2)
                t = i % 2
                if i == 0:
                    act.copy(FZ, b[:, :]).then_inc(s_pe, 1)
                elif i == 1:
                    act.copy(HQ[:, :], b[:, :]).then_inc(s_pe, 1)
                elif i in (2, 3):
                    act.wait_ge(s_pad, l + 1)
                    act.copy(MR[:, 2 * t:2 * t + 2, CK - 1:], two).then_inc(s_pe, 1)
                elif i in (4, 5):
                    act.mul(FQ[:, 2 * t:2 * t + 2, :], two, SCALE).then_inc(s_pe, 1)
                elif i in (6, 7):
                    act.copy(FK[:, 2 * t:2 * t + 2, :], two).then_inc(s_pe, 1)
                elif i in (8, 9):
                    act.copy(FV[:, :, 256 * t:256 * t + 256], two).then_inc(s_pe, 1)
                else:
                    dst = (VM[:, :, :, 0:DH], G2[:, :, NH:, :],
                           HV[:, :, :].rearrange("p t (h d) -> p t h d", h=NH), G2[:, :, 0:NH, :])[i - 10]
                    act.copy(dst, b[:, :].rearrange("p (t h d) -> p t h d", t=T, h=NH)).then_inc(s_pe, 1)
                if i + 2 < NHALF:
                    weights_high(l, i + 2)

            def weights_high(l, i):
                u = unit_base[l] + i // 2
                act.wait_ge(w_loaded[slot_of[u]], LOADED * turn_of[u])
                act.copy(winh[:, i % 2, :, :], half_columns(u, i % 2)).then_inc(s_wih, 1)

            def turned_high(l, dst, n):
                for b in range(4):
                    t, c = b // 2, 4 * (b % 2)
                    act.wait_ge(s_hT, n + b + 1)
                    act.copy(dst[:, c:c + 4, t * P:(t + 1) * P], hT[:, c:c + 4, t * P:(t + 1) * P]).then_inc(s_hTh, 1)

            def log1p_exp_neg_abs(dst, src, s, v, bias=None):
                if bias is None:
                    act.activation(dst, src, ACT.Abs).then_inc(s, 1)
                else:
                    for c in range(2):
                        ins = act.activation(dst[:, 256 * c:256 * c + 256], src[:, 256 * c:256 * c + 256], ACT.Abs,
                                             bias=bias[:, c:c + 1])
                    ins.then_inc(s, 1)
                act.wait_ge(s, v + 1)
                act.activation(dst, dst, ACT.Exp, scale=-1.0).then_inc(s, 1)
                act.wait_ge(s, v + 2)
                act.activation(dst, dst, ACT.Ln, bias=1.0).then_inc(s, 1)

            def attn_exp(l, g):
                act.wait_ge(s_nx, 3 * l + g + 1)
                n, w = (4, P) if g == 0 else (2, SEQ)
                if g == 2:
                    act.wait_ge(s_tp, 6 * l + 2)
                for p in range(2):
                    for c in range(n):
                        ins = act.activation(PP[g % 2][:, (p * n + c) * w:(p * n + c + 1) * w], ps[4 + p][:, c * w:(c + 1) * w],
                                             ACT.Exp, bias=nmx[:, g, p * n + c:p * n + c + 1],
                                             accum_out=rs[:, g, 0, p * n + c:p * n + c + 1])
                ins.then_inc(s_ex, 1)

            def attn_turned(l, g):
                for p in range(2):
                    act.wait_ge(s_tp, 6 * l + 2 * g + p + 1)
                    if g:
                        act.wait_ge(s_pv, 3 * l + g)
                    act.copy(PT[:, p * 512:p * 512 + 512], ps[6][:, :]).then_inc(s_te, 1)

            def attn_out(l, g):
                act.wait_ge(s_pv, 3 * l + g + 1)
                if g == 0:
                    act.copy(mixT[:, 4:8, 0:P], ps[7][:, :].rearrange("p (c t) -> p c t", c=4)).then_inc(s_fo, 1)
                else:
                    act.copy(mixT[:, 2 + 2 * g:4 + 2 * g, P:SEQ],
                             ps[7][:, 0:256].rearrange("p (c t) -> p c t", c=2)).then_inc(s_fo, 1)

            for l in range(DEPTH):
                square_sums(2 * l)
                if l == 0:
                    act.wait_ge(s_lb, 1)
                    log1p_exp_neg_abs(LB[:, 1, :], LB[:, 0, :], s_lba, 0)
                if l:
                    weights_high(l, 0)
                turned_high(l, hTh, 8 * l)
                if not l:
                    weights_high(l, 0)
                weights_high(l, 1)
                act.wait_ge(s_gv, l + 1)
                log1p_exp_neg_abs(GA[:, 3, :, :], GA[:, 0, :, :], s_ga, 3 * l)
                evacuate(l, 0)
                act.wait_ge(s_pe, NHALF * l + 1)
                h1 = 3 * l
                log1p_exp_neg_abs(TMP, FZ, s_h1, h1)
                evacuate(l, 1)
                act.wait_ge(s_h2, (2, 4)[l])
                if l == 0:
                    act.activation(HK[:, :], NK, ACT.Exp, scale=-1.0).then_inc(s_hk, 1)
                else:
                    for c in range(2):
                        ins = act.activation(HK[:, 256 * c:256 * c + 256], NK[:, 256 * c:256 * c + 256], ACT.Exp,
                                             scale=-1.0, bias=LB[:, 3, c:c + 1])
                    ins.then_inc(s_hk, 1)
                    log1p_exp_neg_abs(TMP, LS, s_h1, h1 + 3, bias=LB[:, 4, :])
                for k in range(STEPS):
                    if 1 <= k < LEVELS:
                        act.wait_ge(s_d0, (LEVELS - 1) * l + k)
                        act.activation(DX[:, k % 2, :], DX[:, k % 2, :], ACT.Abs).then_inc(s_dxa, 1)
                        act.wait_ge(s_dxa, (LEVELS - 1) * l + k)
                        act.activation(DX[:, k % 2, :], DX[:, k % 2, :], ACT.Exp, scale=-1.0).then_inc(s_dx, 1)
                    if k >= 8 and k - 8 < 3:
                        attn_exp(l, k - 8)
                    evacuate(l, k + 2)
                    if k == 4:
                        act.wait_ge(s_m, l + 1)
                        act.activation(em[:, :, :], bb[:, :, :], ACT.Exp, scale=-1.0).then_inc(s_em, 1)
                    if k == 6:
                        act.wait_ge(s_e0, 8 * (l + 1))
                        act.activation(ER[:, :], ER[:, :], ACT.Exp).then_inc(s_e, 1)
                    if 9 <= k:
                        attn_out(l, k - 9)
                    if k >= 8 and k - 8 < 3:
                        attn_turned(l, k - 8)
                    if k == 8:
                        act.wait_ge(s_cv, 4 * CK * (l + 1))
                        act.activation(MC[:, :, :], MC[:, :, :], ACT.Silu).then_inc(s_mc, 1)
                act.wait_ge(s_pe, NHALF * (l + 1))
                act.activation(G2[:, :, 0:NH, :], G2[:, :, 0:NH, :], ACT.Silu)
                act.activation(G2[:, :, NH:, :], G2[:, :, NH:, :], ACT.Tanh, scale=0.5).then_inc(s_gr, 1)
                act.wait_ge(s_ho, l + 1)
                act.copy(OM[:, :, 0:NH, :], ps[0][:, :].rearrange("p (t h d) -> p t h d", t=T, h=NH)).then_inc(s_oc, 1)
                for t in range(T):
                    act.wait_ge(s_num, T * l + t + 1)
                    act.activation(dn[:, 0, t, :], ps[1 + t][:, 0:NH * 65].rearrange("p (h e) -> p h e", h=NH)[:, :, DH],
                                   ACT.Abs).then_inc(s_dn, 1)
                act.wait_ge(s_oc, l + 1)
                for t in range(T):
                    act.wait_ge(s_oh, T * l + t + 1)
                    act.activation(SQ[:, t, :, :], OM[:, t, :, :], ACT.Square).then_inc(s_sq, 1)
                act.wait_ge(s_mt, T * l + 1)
                act.copy(mixT[:, 0:4, 0:P], ps[3][:, :].rearrange("p (c t) -> p c t", c=4)).then_inc(s_me, 1)

                square_sums(2 * l + 1)
                if l == 0:
                    def gate_up_high(i):
                        for r, w in enumerate(block_weights(i)[0:2]):
                            u = DENSE0 + 3 * (i // 4) + r
                            act.wait_ge(w_loaded[slot_of[u]], LOADED * turn_of[u])
                            if i >= 2:
                                act.wait_ge(s_gu, i - 1)
                            act.copy(guh[:, i % 2, r, :, :], w).then_inc(s_guh, 1)

                    gate_up_high(0)
                    turned_high(l, dTh, 4)
                    gate_up_high(1)
                    for i in range(NB):
                        act.wait_ge(s_gu, i + 1)
                        if i >= 4:
                            act.wait_ge(s_ht, i - 3)
                        act.activation(SG[i % 4], ps[i % 4][:, 0:SEQ], ACT.Silu).then_inc(s_sg, 1)
                        u = DENSE0 + 3 * (i // 4) + 2
                        act.wait_ge(w_loaded[slot_of[u]], LOADED * turn_of[u])
                        if i >= 2:
                            act.wait_ge(s_dd, i - 1)
                        act.copy(dwh[:, i % 2, :], block_weights(i)[2]).then_inc(s_dwh, 1)
                        act.wait_ge(s_ht, i + 1)
                        act.copy(HTh[:, i % 2, :], HT[i % 4]).then_inc(s_hdh, 1)
                        if i + 2 < NB:
                            gate_up_high(i + 2)

            def tokens_high(j):
                for b in range(2):
                    act.wait_ge(s_gx, 2 * j + b + 1)
                    act.copy(xeh[:, 4 * b:4 * b + 4, :], ps[2 + b][:, :].rearrange("p (c s) -> p c s", c=4)).then_inc(s_xh, 1)

            def out_high(j):
                act.wait_ge(s_sTc, j + 1)
                for n in range(2):
                    act.activation(yeh[:, n * BANK:(n + 1) * BANK], ps[4 + n][:, :], ACT.Copy,
                                   scale=gslot[:, 0:1]).then_inc(s_yh, 1)

            def piece_high(j, q):
                act.wait_ge(raw_loaded[q % RAW], 16 * (NPC // RAW) * j + 16 * (q // RAW + 1))
                act.wait_ge(s_used, nth_use(j, q - SPLIT))
                act.copy(high[:, q % SPLIT, :], raw[:, q % RAW, :]).then_inc(s_hi, 1)

            for q in range(SPLIT):
                piece_high(0, q)
            act.wait_ge(s_rt, RT_DIFF)
            act.activation(RV[:, 3, :], RV[:, 2, :], ACT.Exp).then_inc(s_rx, 1)
            tokens_high(0)
            act.wait_ge(s_jl, 1)
            last = act.value_load(jobs[0:1, 17:18], min_val=1, max_val=MAXJOBS - 1)

            def job(j, is_last=False):
                out_high(j)
                for q in range(SPLIT, NPC):
                    piece_high(j, q)
                    p = q - (SPLIT - 1)
                    if q == 9:
                        act.wait_ge(s_sT, j + 1)
                        act.copy(gslot[:, :], ps[7][:, SEQ:SEQ + 1])
                        act.copy(selT[:, :], ps[7][:, 0:SEQ]).then_inc(s_sTc, 1)
                    if ORDER[p][0] == "gate" and ORDER[p][2] == 1:
                        c = ORDER[p][1]
                        act.wait_ge(s_used, nth_use(j, p))
                        if c >= 2:
                            act.wait_ge(s_eh, NCH * j + c - 1)
                        act.activation(sil[:, c % 2, :], ps[2 * (c % 2)][:, :], ACT.Silu).then_inc(s_es, 1)
                        if c:
                            act.wait_ge(s_et, NCH * j + c)
                            act.copy(hdh[:, (c - 1) % 2, :], ps[6][:, :]).then_inc(s_hh, 1)
                act.wait_ge(s_et, NCH * j + NCH)
                act.copy(hdh[:, (NCH - 1) % 2, :], ps[6][:, :]).then_inc(s_hh, 1)
                if not is_last:
                    tokens_high(j + 1)
                    for q in range(SPLIT):
                        piece_high(j + 1, q)

            with act.Fori(0, last) as j:
                job(j)
            job(last, is_last=True)
            act.wait_ge(s_used, nth_use(last, NPC - 1))
            out_high(last + 1)
            square_sums(2 * DEPTH, last + 1)

        @block.vector
        def _(dve):
            def bc(ap, shape):
                return ap.to_broadcast(shape)

            def normalise(i):
                dve.wait_ge(s_rms, i + 1)
                for t in range(T):
                    dve.tensor_scalar(XN[:, t, :], X[:, t, :], st[:, i, 1, t:t + 1], None, ALU.mult).then_inc(s_xn, 1)

            def turned(i, gain):
                for b in range(4):
                    t, c = b // 2, 4 * (b % 2)
                    dve.wait_ge(s_xt, 4 * i + b + 1)
                    dve.tensor_tensor(hT[:, c:c + 4, t * P:(t + 1) * P], ps[b][:, :].rearrange("p (c t) -> p c t", c=4),
                                      bc(gain[:, c:c + 4].unsqueeze(2), [P, 4, P]), ALU.mult).then_inc(s_hT, 1)

            def turned_low(high_, low_, n):
                for b in range(4):
                    t, c = b // 2, 4 * (b % 2)
                    v = (slice(None), slice(c, c + 4), slice(t * P, (t + 1) * P))
                    dve.wait_ge(s_hTh, n + b + 1)
                    dve.tensor_tensor(low_[v], hT[v], high_[v].bitcast(F32), ALU.subtract).then_inc(s_hTl, 1)

            def gate_up_low(i):
                for r, w in enumerate(block_weights(i)[0:2]):
                    dve.wait_ge(s_guh, 2 * i + r + 1)
                    ins = dve.tensor_tensor(gul[:, i % 2, r, :, :], w, guh[:, i % 2, r, :, :].bitcast(F32), ALU.subtract)
                ins.then_inc(s_gul, 1)

            def weights_low(l, i):
                dve.wait_ge(s_wih, NHALF * l + i + 1)
                dve.tensor_tensor(winl[:, i % 2, :, :], half_columns(unit_base[l] + i // 2, i % 2),
                                  winh[:, i % 2, :, :].bitcast(F32), ALU.subtract).then_inc(s_wil, 1)

            def add_residual(ready):
                for n in range(2):
                    for t in range(T):
                        ready(n, t)
                        xs = X[:, t, n * BANK:(n + 1) * BANK]
                        dve.tensor_tensor(xs, xs, ps[4 + 2 * n + t][:, :], ALU.add).then_inc(s_res, 1)

            def level_difference(l, k):
                if k >= 3:
                    dve.wait_ge(s_kd, (LEVELS - 1) * l + k - 2)
                elif l:
                    dve.wait_ge(s_kd, (LEVELS - 1) * l)
                d = DX[:, k % 2, :]
                if k < 8:
                    v, h = halves(B[:, :], k), 2 ** (k - 1)
                    dve.tensor_tensor(halves(d, k), v, bc(v[:, :, h - 1:h], [P, 512 // (2 * h), 2 * h]), ALU.subtract)\
                        .then_inc(s_d0, 1)
                else:
                    v = B[:, :].rearrange("p (c t s) -> p c t s", c=2, t=T)
                    w = d.rearrange("p (c t s) -> p c t s", c=2, t=T)
                    dve.tensor_tensor(w[:, :, 0, :], v[:, :, 0, :], bc(v[:, :, 0, P - 1:P], [P, 2, P]), ALU.subtract)
                    dve.tensor_copy(w[:, :, 1, :], v[:, :, 1, :]).then_inc(s_d0, 1)

            def level_queries(l, k):
                dve.wait_ge(s_dx, (LEVELS - 1) * l + k)
                if k >= 3:
                    dve.wait_ge(s_lp, LEVELS * l + k - 1)
                dve.tensor_tensor(QD[:, k % 2, :], HQ[:, :], DX[:, k % 2, :], ALU.mult).then_inc(s_qd, 1)

            def level_copy(l, k):
                dve.wait_ge(s_lp, LEVELS * l + k + 1)
                if k == 0:
                    dve.wait_ge(s_pad, l + 1)
                for p in range(2):
                    if k < 8:
                        ins = dve.copy_predicated(SC[:, p, :, :], bc(LM[:, k, :].bitcast(I32).unsqueeze(1), [P, 4, P]),
                                                  ps[2 + p][:, :].rearrange("p (b t) -> p b t", b=4))
                    else:
                        ins = dve.tensor_copy(SX[:, p, :, :], ps[2 + p][:, 0:256].rearrange("p (c t) -> p c t", c=2))
                ins.then_inc(s_lc, 1)

            def attn_max(l, g):
                n, w = (4, P) if g == 0 else (2, SEQ)
                dve.wait_ge(s_S, 3 * l + g + 1)
                for p in range(2):
                    ins = dve.tensor_reduce(nmx[:, g, p * n:(p + 1) * n], ps[4 + p][:, :].rearrange("p (c s) -> p c s", c=n),
                                            AX.X, ALU.max)
                ins.then_inc(s_mx, 1)
                dve.wait_ge(s_mx, 3 * l + g + 1)
                dve.tensor_scalar(nmx[:, g, 0:2 * n], nmx[:, g, 0:2 * n], -1.0, None, ALU.mult).then_inc(s_nx, 1)

            def attn_weights(l, g):
                n, w = (8, P) if g == 0 else (4, SEQ)
                dve.wait_ge(s_ex, 3 * l + g + 1)
                dve.reciprocal(rs[:, g, 1, 0:n], rs[:, g, 0, 0:n]).then_inc(s_rr, 1)
                dve.wait_ge(s_rr, 3 * l + g + 1)
                v = PP[g % 2].rearrange("p (m w) -> p m w", m=n)
                dve.tensor_tensor(v, v, bc(rs[:, g, 1, 0:n].unsqueeze(2), [P, n, w]), ALU.mult).then_inc(s_pn, 1)

            def convolve(l, j):
                dve.wait_ge(s_pe, NHALF * l + 4)
                dve.wait_ge(s_pad, l + 1)
                if j:
                    dve.wait_ge(s_cv, 4 * (CK * l + j))
                for c in range(4):
                    w = PCc[:, l, j, c:c + 1]
                    if j == 0:
                        ins = dve.tensor_scalar(MC[:, c, :], MR[:, c, 0:SEQ], w, None, ALU.mult)
                    else:
                        ins = dve.scalar_tensor_tensor(out=MC[:, c, :], in0=MR[:, c, j:j + SEQ], scalar=w,
                                                       in1=MC[:, c, :], op0=ALU.mult, op1=ALU.add)
                    ins.then_inc(s_cv, 1)

            def lower_bound():
                dve.wait_ge(s_lba, 3)
                dve.wait_ge(s_lb, 1)
                dve.scalar_tensor_tensor(out=LB[:, 2, :], in0=LB[:, 0, :], scalar=0.0, in1=LB[:, 1, :],
                                         op0=ALU.min, op1=ALU.subtract).then_inc(s_lb, 1)
                dve.scalar_tensor_tensor(out=LBT[:, 0, :], in0=LB[:, 0, :], scalar=0.0, in1=LB[:, 1, :],
                                         op0=ALU.max, op1=ALU.add).then_inc(s_lb, 1)
                dve.wait_ge(s_lb, 3)
                dve.tensor_scalar(LB[:, 3, :], LBT[:, 0, :], -1.0, None, ALU.mult).then_inc(s_lb, 1)
                dve.wait_ge(s_lb, 4)
                dve.tensor_tensor(LB[:, 4, :], LB[:, 3, :], LB[:, 2, :], ALU.subtract).then_inc(s_lb, 1)

            dve.wait_ge(s_prT, 1)
            dve.tensor_copy(PC[:, :], ps[6][:, 0:68]).then_inc(s_pc, 1)
            dve.wait_ge(s_pc, 1)
            dve.tensor_tensor(LB[:, 0, :], PCl[:, 1, :], PCl[:, 0, :], ALU.subtract).then_inc(s_lb, 1)

            for l in range(DEPTH):
                normalise(2 * l)
                if l:
                    weights_low(l, 0)
                turned(2 * l, PCa[:, l, :])
                turned_low(hTh, hTl, 8 * l)
                if not l:
                    weights_low(l, 0)
                if l == 0:
                    lower_bound()
                weights_low(l, 1)
                dve.wait_ge(s_par, NPAR)
                dve.wait_ge(s_gp, l + 1)
                dve.tensor_tensor(GA[:, 0, :, :], ps[7][:, 0:32].rearrange("p (t g) -> p t g", t=T),
                                  bc(GB[:, l, :].unsqueeze(1), [P, T, 16]), ALU.add).then_inc(s_gv, 1)
                dve.wait_ge(s_gv, l + 1)
                dve.wait_ge(s_ga, 3 * l + 3)
                dve.scalar_tensor_tensor(out=GA[:, 1, :, :], in0=GA[:, 0, :, :], scalar=0.0, in1=GA[:, 3, :, :],
                                         op0=ALU.min, op1=ALU.subtract).then_inc(s_ls, 1)
                dve.wait_ge(s_ls, 2 * l + 1)
                dve.tensor_scalar(GA[:, 2, :, :], GA[:, 1, :, :], -1.0, None, ALU.mult).then_inc(s_ls, 1)
                weights_low(l, 2)
                dve.wait_ge(s_h1, 3 * l + 3)
                dve.wait_ge(s_pe, NHALF * l + 1)
                h2 = 2 * l
                dve.scalar_tensor_tensor(out=LS, in0=FZ, scalar=0.0, in1=TMP, op0=ALU.min, op1=ALU.subtract).then_inc(s_h2, 1)
                dve.scalar_tensor_tensor(out=NK, in0=FZ, scalar=0.0, in1=TMP, op0=ALU.max, op1=ALU.add).then_inc(s_h2, 1)
                dve.wait_ge(s_cb, l + 1)
                cb = ps[7][:, 32:40].rearrange("p (t h) -> p t h", t=T)
                dve.tensor_tensor(aa[:, :, :], GA[:, 0, :, 0:NH], cb, ALU.subtract).then_inc(s_a, 1)
                dve.tensor_copy(bb[:, :, :], cb).then_inc(s_a, 1)
                lf = LS
                if l:
                    dve.wait_ge(s_h2, h2 + 2)
                    dve.wait_ge(s_lb, 5)
                    for c in range(2):
                        dve.tensor_scalar(FZ[:, 256 * c:256 * c + 256], LS[:, 256 * c:256 * c + 256], LB[:, 3, c:c + 1],
                                          LB[:, 2, c:c + 1], ALU.add, ALU.max).then_inc(s_h2, 1)
                    weights_low(l, 3)
                    dve.wait_ge(s_h2, h2 + 4)
                    dve.wait_ge(s_h1, 9)
                    dve.tensor_tensor(LF[:, :], FZ, TMP, ALU.add).then_inc(s_h2, 1)
                    lf = LF[:, :]
                    dve.wait_ge(s_h2, h2 + 5)
                else:
                    dve.wait_ge(s_h2, 2)
                dve.wait_ge(s_cst, NCONST)
                for c in range(4):
                    v = slice(c * P, (c + 1) * P)
                    dve.tensor_tensor_scan(B[:, v], lf[:, v], MM[:, P:2 * P], 0.0, ALU.add, ALU.add).then_inc(s_b, 1)
                dve.wait_ge(s_b, 4 * l + 4)
                if not l:
                    weights_low(l, 3)
                level_difference(l, 1)

                for k in range(STEPS):
                    if 1 <= k < LEVELS:
                        level_queries(l, k)
                        if k + 1 < LEVELS:
                            level_difference(l, k + 1)
                    if k == 1:
                        dve.wait_ge(s_aT, l + 1)
                        for t in range(T):
                            v = slice(t * P, (t + 1) * P)
                            if t:
                                dve.wait_ge(s_g, T * l + t)
                            dve.tensor_tensor_scan(gT[:, v], ps[7][0:NH, 64 + t * P:64 + (t + 1) * P], MM[0:NH, P:2 * P],
                                                   0.0 if t == 0 else gT[:, t * P - 1:t * P], ALU.max, ALU.max).then_inc(s_g, 1)
                    if k == 4:
                        dve.wait_ge(s_gi, l + 1)
                        dve.wait_ge(s_a, 2 * l + 2)
                        dve.tensor_tensor(bb[:, :, :], bb[:, :, :], ps[7][:, 400:408].rearrange("p (t h) -> p t h", t=T),
                                          ALU.add).then_inc(s_m, 1)
                    if k == 6:
                        dve.wait_ge(s_gb, l + 1)
                        dve.wait_ge(s_cv, 4 * CK * (l + 1))
                        for h in range(NH):
                            g = ps[4 + h // 2][:, (h % 2) * SEQ:(h % 2 + 1) * SEQ]
                            dve.scalar_tensor_tensor(out=E[:, h // 2, h % 2, 0:SEQ], in0=g, scalar=aa[:, 0, h:h + 1],
                                                     in1=MM[:, :], op0=ALU.add, op1=ALU.min).then_inc(s_e0, 1)
                            dve.scalar_tensor_tensor(out=E[:, h // 2, h % 2, SEQ:], in0=g[:, P:], scalar=aa[:, 1, h:h + 1],
                                                     in1=MM[:, 0:P], op0=ALU.add, op1=ALU.min).then_inc(s_e0, 1)
                    if 8 <= k < 11:
                        attn_max(l, k - 8)
                    if k == 0:
                        level_copy(l, 0)
                    if 2 <= k <= LEVELS:
                        level_copy(l, k - 1)
                    if 2 <= k < 2 + CK:
                        convolve(l, k - 2)
                    if 8 <= k < 11:
                        attn_weights(l, k - 8)
                    if k + 4 < NHALF:
                        weights_low(l, k + 4)
                dve.wait_ge(s_e, l + 1)
                for r, b0, v in ((0, 2, slice(0, SEQ)), (1, 4, slice(SEQ, SEQ + P))):
                    dve.wait_ge(s_qk, 2 * l + r + 1)
                    n = v.stop - v.start
                    for q in range(2):
                        dve.scalar_tensor_tensor(out=E[:, :, q, v], in0=ps[b0 + q][:, 0:2 * n].rearrange("p (c t) -> p c t", c=2),
                                                 scalar=SCALE, in1=E[:, :, q, v], op0=ALU.mult, op1=ALU.mult).then_inc(s_w, 1)
                for t in range(T):
                    dve.wait_ge(s_dn, T * l + t + 1)
                    dve.wait_ge(s_em, l + 1)
                    dve.tensor_tensor(dn[:, 1, t, :], dn[:, 0, t, :], em[:, t, :], ALU.max).then_inc(s_dr, 1)
                    dve.wait_ge(s_dr, 4 * l + 2 * t + 1)
                    dve.reciprocal(dn[:, 1, t, :], dn[:, 1, t, :]).then_inc(s_dr, 1)
                    dve.wait_ge(s_dr, 4 * l + 2 * t + 2)
                    dve.tensor_tensor(OM[:, t, NH:, :], ps[1 + t][:, 0:NH * 65].rearrange("p (h e) -> p h e", h=NH)[:, :, 0:DH],
                                      bc(dn[:, 1, t, :].unsqueeze(2), [P, NH, DH]), ALU.mult).then_inc(s_oh, 1)
                for t in range(T):
                    dve.wait_ge(s_sq, T * l + t + 1)
                    dve.tensor_reduce(hs[:, 0, t, :], SQ[:, t, :, :], AX.X, ALU.add).then_inc(s_hs, 1)
                for t in range(T):
                    dve.wait_ge(s_hr, T * l + t + 1)
                    dve.wait_ge(s_oh, T * (l + 1))
                    dve.tensor_tensor(OM[:, t, :, :], OM[:, t, :, :], bc(hs[:, 1, t, :].unsqueeze(2), [P, 2 * NH, DH]),
                                      ALU.mult).then_inc(s_on, 1)
                    dve.wait_ge(s_on, T * l + t + 1)
                    dve.wait_ge(s_g2, 2 * l + 2)
                    dve.tensor_tensor(OM[:, t, :, :], OM[:, t, :, :], G2[:, t, :, :], ALU.mult).then_inc(s_og, 1)
                dve.wait_ge(s_mt, T * l + 2)
                dve.tensor_copy(mixT[:, 0:4, P:SEQ], ps[0][:, :].rearrange("p (c t) -> p c t", c=4)).then_inc(s_me1, 1)
                add_residual(lambda n, t: dve.wait_ge(s_wo, 4 * l + 2 * n + t + 1))

                normalise(2 * l + 1)
                if l == 0:
                    gate_up_low(0)
                turned(2 * l + 1, PCf[:, l, :])
                if l == 0:
                    turned_low(dTh, dTl, 4)

                    gate_up_low(1)
                    for i in range(NB):
                        dve.wait_ge(s_dwh, i + 1)
                        dve.tensor_tensor(dwl[:, i % 2, :], block_weights(i)[2], dwh[:, i % 2, :].bitcast(F32),
                                          ALU.subtract).then_inc(s_dwl, 1)
                        dve.wait_ge(s_sg, i + 1)
                        dve.tensor_tensor(HT[i % 4], SG[i % 4], ps[i % 4][:, SEQ:2 * SEQ], ALU.mult).then_inc(s_ht, 1)
                        dve.wait_ge(s_hdh, i + 1)
                        dve.tensor_tensor(HTl[:, i % 2, :], HT[i % 4], HTh[:, i % 2, :].bitcast(F32), ALU.subtract)\
                            .then_inc(s_hdl, 1)
                        if i + 2 < NB:
                            gate_up_low(i + 2)
                    add_residual(lambda n, t: dve.wait_ge(s_dd, NB))

            def piece_low(j, q):
                dve.wait_ge(s_hi, nth_piece(j, q))
                dve.tensor_tensor(low[:, q % SPLIT, :], raw[:, q % RAW, :], high[:, q % SPLIT, :].bitcast(F32),
                                  ALU.subtract).then_inc(s_lo, 1)

            for q in range(SPLIT):
                piece_low(0, q)

            def select(j, rows):
                for t in range(T):
                    ins = dve.tensor_scalar(selS[:, t, :], iota[:, :], rows(t), None, ALU.is_equal)
                ins.then_inc(s_sel, 1)

            def job_gates(j):
                for t in range(T):
                    ins = dve.tensor_copy(gcol[:, t:t + 1], RC[:, 3, t, bass.ds(j, 1)])
                ins.then_inc(s_gc, 1)

            step = [0]

            def then(ins):
                ins.then_inc(s_rt, 1)
                step[0] += 1
                dve.wait_ge(s_rt, step[0])

            def row(r):
                return RT[:, r, :].rearrange("p (t e) -> p t e", t=T)

            def top(src, eq, cs, first, v):
                then(dve.tensor_reduce(v, row(src), AX.X, ALU.max))
                then(dve.tensor_tensor(row(eq), row(src), bc(v.unsqueeze(2), [P, T, NE]), ALU.is_equal))
                for t in range(T):
                    then(dve.tensor_tensor_scan(row(cs)[:, t, :], row(eq)[:, t, :], MM[:, P:P + NE], 0.0, ALU.add, ALU.add))
                then(dve.scalar_tensor_tensor(out=row(first), in0=row(cs), scalar=1.0, in1=row(eq),
                                              op0=ALU.is_equal, op1=ALU.mult))

            dve.wait_ge(s_lg, 1)
            then(dve.tensor_copy(RT[:, 0, :], ps[7][:, 0:16]))
            top(0, 1, 2, 3, RV[:, 0, :])
            then(dve.scalar_tensor_tensor(out=RT[:, 4, :], in0=RT[:, 3, :], scalar=-BIG, in1=RT[:, 0, :],
                                          op0=ALU.mult, op1=ALU.add))
            top(4, 5, 6, 7, RV[:, 1, :])
            then(dve.tensor_tensor(RT[:, 10, :], RT[:, 3, :], RT[:, 7, :], ALU.add))
            assert step[0] == RT_CHOSEN
            then(dve.tensor_tensor(RV[:, 2, :], RV[:, 1, :], RV[:, 0, :], ALU.subtract))
            assert step[0] == RT_DIFF
            dve.wait_ge(s_rk, 1)
            rank = ps[7][:, 32:48].rearrange("p (t e) -> p t e", t=T)
            slots = RC[:, 0, :, :].rearrange("p t (e b) -> p t e b", b=2)
            gates = RC[:, 1, :, :].rearrange("p t (e b) -> p t e b", b=2)
            active = JB[:, 0, :].rearrange("p (e b) -> p e b", b=2)
            for b in range(2):
                then(dve.scalar_tensor_tensor(out=slots[:, :, :, b], in0=rank, scalar=-float(P * b), in1=row(10),
                                              op0=ALU.add, op1=ALU.mult))
            then(dve.tensor_scalar(RC[:, 0, :, :], RC[:, 0, :, :], -1.0, None, ALU.add))
            select(0, lambda t: RC[:, 0, t, 0:1])
            for b in range(2):
                then(dve.tensor_scalar(active[:, :, b], ps[7][:, 48:56], float(P * b), None, ALU.is_gt))
            then(dve.memset(JB[:, 0, 0:1], 1.0))
            then(dve.tensor_tensor_scan(JB[:, 1, :], JB[:, 0, :], MM[:, P:P + 16], 0.0, ALU.add, ALU.add))
            oh = [OH[:, i, :].rearrange("p (j c) -> p j c", c=16) for i in range(2)]
            full = [P, 16, 16]
            then(dve.tensor_tensor(oh[0], bc(JB[:, 1, :].unsqueeze(1), full), bc(cidx[:, 0, :].unsqueeze(2), full), ALU.is_equal))
            then(dve.tensor_tensor(oh[0], oh[0], bc(JB[:, 0, :].unsqueeze(1), full), ALU.mult))

            def by_job(dst, src):
                then(dve.tensor_tensor(oh[1], oh[0], bc(src.unsqueeze(1), full), ALU.mult))
                then(dve.tensor_reduce(dst, oh[1], AX.X, ALU.add))

            by_job(JB[:, 2, :], cidx[:, 1, :])
            then(dve.tensor_copy(jobs[:, 0:16], JB[:, 2, :]))
            dve.tensor_copy(jobs[:, 16:17], JB[:, 1, 15:16])
            dve.tensor_scalar(jobs[:, 17:18], JB[:, 1, 15:16], -1.0, None, ALU.add).then_inc(s_jl, 1)
            dve.wait_ge(s_rx, 1)
            then(dve.tensor_scalar(RV[:, 4, :], RV[:, 3, :], 1.0, None, ALU.add))
            then(dve.reciprocal(RV[:, 5, :], RV[:, 4, :]))
            then(dve.tensor_tensor(RV[:, 6, :], RV[:, 3, :], RV[:, 5, :], ALU.mult))
            then(dve.tensor_tensor(row(8), row(3), bc(RV[:, 5, :].unsqueeze(2), [P, T, NE]), ALU.mult))
            then(dve.tensor_tensor(row(9), row(7), bc(RV[:, 6, :].unsqueeze(2), [P, T, NE]), ALU.mult))
            then(dve.tensor_tensor(RT[:, 8, :], RT[:, 8, :], RT[:, 9, :], ALU.add))
            for b in range(2):
                then(dve.tensor_copy(gates[:, :, :, b], row(8)))
            def tokens_low(j, banks=(0, 1)):
                for b in banks:
                    dve.wait_ge(s_xh, 2 * j + b + 1)
                    dve.tensor_tensor(xel[:, 4 * b:4 * b + 4, :], ps[2 + b][:, :].rearrange("p (c s) -> p c s", c=4),
                                      xeh[:, 4 * b:4 * b + 4, :].bitcast(F32), ALU.subtract).then_inc(s_xl, 1)

            def out_low(j):
                for n in range(2):
                    dve.wait_ge(s_yh, 2 * j + n + 1)
                    v = slice(n * BANK, (n + 1) * BANK)
                    dve.scalar_tensor_tensor(out=yel[:, v], in0=ps[4 + n][:, :], scalar=gslot[:, 0:1],
                                             in1=yeh[:, v].bitcast(F32), op0=ALU.mult, op1=ALU.subtract).then_inc(s_yl, 1)

            def add_results(j, i, last=False):
                t, n = i // 2, i % 2
                b = ps[i] if last else ps[7]
                dve.wait_ge(s_cz, 4 * j + i + 1)
                xs = X[:, t, n * BANK:(n + 1) * BANK]
                dve.tensor_tensor(xs, xs, b[:, :], ALU.add).then_inc(s_ca, 1)

            def hidden_low(j, c):
                dve.wait_ge(s_hh, NCH * j + c + 1)
                dve.tensor_tensor(hdl[:, c % 2, :], ps[6][:, :], hdh[:, c % 2, :].bitcast(F32), ALU.subtract).then_inc(s_hl, 1)

            dve.memset(gslot[:, :], 0.0)
            dve.memset(selT[:, :].bitcast(F32), 0.0).then_inc(s_sTc, 1)
            dve.wait_ge(s_rt, step[0])
            for t in range(T):
                by_job(RC[:, 2, t, :], RC[:, 0, t, :])
                tokens_low(0, banks=(t,))
            for t in range(T):
                by_job(RC[:, 3, t, :], RC[:, 1, t, :])
            job_gates(0)
            dve.wait_ge(s_jl, 1)
            last = dve.value_load(jobs[0:1, 17:18], min_val=1, max_val=MAXJOBS - 1)

            def job(j, is_last=False):
                out_low(j)
                for q in range(SPLIT, NPC):
                    piece_low(j, q)
                    p = q - (SPLIT - 1)
                    if 0 <= p - 1 < 4:
                        add_results(j, p - 1)
                    if q == 20:
                        dve.wait_ge(s_sT, j + 1)
                        select(j + 1, lambda t: RC[:, 2, t, bass.ds(j + 1, 1)])
                        job_gates(j + 1)
                    if ORDER[p][2] == 1:
                        kind, c, _ = ORDER[p]
                        if kind == "gate" and c:
                            hidden_low(j, c - 1)
                        if kind == "up":
                            dve.wait_ge(s_es, NCH * j + c + 1)
                            dve.wait_ge(s_used, nth_use(j, p))
                            if c >= 2:
                                dve.wait_ge(s_et, NCH * j + c - 1)
                            dve.tensor_tensor(hid[:, c % 2, :], sil[:, c % 2, :], ps[2 * (c % 2) + 1][:, :], ALU.mult)\
                                .then_inc(s_eh, 1)
                hidden_low(j, NCH - 1)
                if not is_last:
                    tokens_low(j + 1)
                    for q in range(SPLIT):
                        piece_low(j + 1, q)

            with dve.Fori(0, last) as j:
                job(j)
            job(last, is_last=True)
            out_low(last + 1)
            for i in range(4):
                add_results(last + 1, i, last=True)
            dve.wait_ge(s_rms, 2 * DEPTH + 1)
            dve.wait_ge(s_fg, 16)
            for t in range(T):
                dve.scalar_tensor_tensor(out=XN[:, t, :], in0=X[:, t, :], scalar=st[:, 2 * DEPTH, 1, t:t + 1], in1=fgain,
                                         op0=ALU.mult, op1=ALU.mult).then_inc(s_fin, 1)

        @block.tensor
        def _(pe):
            def three(o, xh, xl, wh, wl, first, last):
                pe.matmul(o, xh, wh, start=first, stop=False)
                pe.matmul(o, xh, wl, start=False, stop=False)
                return pe.matmul(o, xl, wh, start=False, stop=last)

            def turn(i):
                for b in range(4):
                    t, c0 = b // 2, 4 * (b % 2)
                    pe.wait_ge(s_xn, 2 * i + t + 1)
                    for c in range(4):
                        ins = pe.transpose(ps[b][:, c * P:(c + 1) * P], XN[:, t, (c0 + c) * P:(c0 + c + 1) * P], ident[:, :])
                    ins.then_inc(s_xt, 1)

            def unit(u, k, n):
                pe.wait_ge(w_loaded[slot_of[u]], LOADED * turn_of[u])
                return ring[:, slot_of[u] * SLOT:slot_of[u] * SLOT + k * n].rearrange("p (k n) -> p k n", k=k)

            def project(l, i):
                s = i // 2
                pe.wait_ge(s_hTl, 8 * l + 4)
                pe.wait_ge(s_wil, NHALF * l + i + 1)
                if i >= 2:
                    pe.wait_ge(s_pe, NHALF * l + i - 1)
                b, wh, wl = ps[i % 2], winh[:, i % 2, :, :], winl[:, i % 2, :, :]
                for f in range(2):
                    o, v = b[:, f * SEQ:(f + 1) * SEQ], slice(f * P, (f + 1) * P)
                    for k in range(KD):
                        if FEATURE_MAJOR[s]:
                            ins = three(o, wh[:, k, v], wl[:, k, v], hTh[:, k, :], hTl[:, k, :], k == 0, k == KD - 1)
                        else:
                            ins = three(o, hTh[:, k, v], hTl[:, k, v], wh[:, k, :], wl[:, k, :], k == 0, k == KD - 1)
                ins.then_inc(s_pp, 1)

            def level(l, k):
                if k == 0:
                    pe.wait_ge(s_hk, l + 1)
                    q, kk = HQ[:, :], HK[:, :]
                    if l:
                        pe.wait_ge(s_res, 8)
                else:
                    pe.wait_ge(s_qd, (LEVELS - 1) * l + k)
                    pe.wait_ge(s_kd, (LEVELS - 1) * l + k)
                    pe.wait_ge(s_lc, LEVELS * l + k)
                    q, kk = QD[:, k % 2, :], KDk[:, k % 2, :]
                for c in range(2):
                    for p in range(2):
                        r = slice(DH * p, DH * p + DH)
                        if k < 8:
                            for t in range(T):
                                v = slice(c * SEQ + t * P, c * SEQ + (t + 1) * P)
                                ins = pe.matmul(ps[2 + p][:, (2 * c + t) * P:(2 * c + t + 1) * P], kk[r, v], q[r, v],
                                                start=True, stop=True)
                        else:
                            ins = pe.matmul(ps[2 + p][:, c * P:(c + 1) * P], kk[r, c * SEQ:c * SEQ + P],
                                            q[r, c * SEQ + P:(c + 1) * SEQ], start=True, stop=True)
                ins.then_inc(s_lp, 1)

            def attn_scores(l, g):
                if g == 0:
                    pe.wait_ge(s_e0, 8 * (l + 1))
                    pe.wait_ge(s_pe, NHALF * l + 8)
                    pe.wait_ge(s_ls, 2 * l + 2)
                else:
                    pe.wait_ge(s_ex, 3 * l + g)
                heads = range(NFH) if g == 0 else range(4 * (g - 1), 4 * g)
                w, qt = (P, 0) if g == 0 else (SEQ, 1)
                for h in heads:
                    p, c = h % 2, h // 2
                    r = slice(DH * p, DH * p + DH)
                    o = ps[4 + p][:, (c * w) % BANK:(c * w) % BANK + w]
                    nlf = GA[:, 2, :, 2 * NH + h:2 * NH + h + 1]
                    pe.matmul(o, FQ[r, c, qt * P:(qt + 1) * P], FK[r, c, 0:w], start=True, stop=False)
                    if g:
                        pe.matmul(o[:, P:], nlf[:, 1, :].to_broadcast([P, P]), UO[:, 0:P], start=False, stop=False,
                                  skip_group_check=True)
                    pe.matmul(o[:, w - P:], ident[:, :], NM[:, :], start=False, stop=False, skip_group_check=True)
                    ins = pe.matmul(o, nlf[:, 0, :].to_broadcast([P, P]), UO[:, 0:w], start=False, stop=True)
                ins.then_inc(s_S, 1)

            def attn_turn(l, g):
                pe.wait_ge(s_pn, 3 * l + g + 1)
                for p in range(2):
                    if 2 * g + p:
                        pe.wait_ge(s_te, 6 * l + 2 * g + p)
                    for b in range(4):
                        v = (4 * p + b) * P
                        ins = pe.transpose(ps[6][:, b * P:(b + 1) * P], PP[g % 2][:, v:v + P], ident[:, :])
                    ins.then_inc(s_tp, 1)

            def attn_apply(l, g):
                pe.wait_ge(s_te, 6 * l + 2 * g + 2)
                pe.wait_ge(s_pe, NHALF * l + 10)
                pe.wait_ge(s_em, l + 1)
                if g:
                    pe.wait_ge(s_fo, 3 * l + g)
                heads = range(NFH) if g == 0 else range(4 * (g - 1), 4 * g)
                for h in heads:
                    p, c = h % 2, h // 2 if g == 0 else (h // 2) % 2
                    o = ps[7][DH * p:DH * p + DH, c * P:(c + 1) * P]
                    tiles = 1 if g == 0 else T
                    for t in range(tiles):
                        b = 4 * p + (c if g == 0 else 2 * c + t)
                        ins = pe.matmul(o, FV[:, t, h * DH:(h + 1) * DH], PT[:, b * P:(b + 1) * P],
                                        start=(t == 0), stop=(t == tiles - 1))
                ins.then_inc(s_pv, 1)

            pe.wait_ge(s_cst, 2)
            pe.wait_ge(s_rows, 16 * 4)
            pe.transpose(ps[6][:, 0:68], PR[:, :], ident[0:68, 0:68]).then_inc(s_prT, 1)

            for l in range(DEPTH):
                turn(2 * l)
                pe.wait_ge(s_par, NPAR)
                pe.wait_ge(s_hT, 4 * (2 * l) + 4)
                for t in range(T):
                    for k in range(KD):
                        ins = pe.matmul(ps[7][:, t * 16:(t + 1) * 16], hT[:, k, t * P:(t + 1) * P], WG[:, l, k, :],
                                        start=(k == 0), stop=(k == KD - 1))
                ins.then_inc(s_gp, 1)
                project(l, 0)
                project(l, 1)
                pe.wait_ge(s_cst, NCONST)
                pe.wait_ge(s_ls, 2 * l + 1)
                pe.matmul(ps[7][:, 32:36], UO[:, 0:P], GA[:, 1, 0, NH:2 * NH], start=True, stop=True)
                pe.matmul(ps[7][:, 36:40], UO[:, P:2 * P], GA[:, 1, 0, NH:2 * NH], start=True, stop=False)
                pe.matmul(ps[7][:, 36:40], UO[:, 0:P], GA[:, 1, 1, NH:2 * NH], start=False, stop=True).then_inc(s_cb, 1)
                for k in range(STEPS):
                    if k == 1:
                        pe.wait_ge(s_a, 2 * l + 2)
                        for t in range(T):
                            ins = pe.transpose(ps[7][0:NH, 64 + t * P:64 + (t + 1) * P], aa[:, t, :], ident[:, :])
                        ins.then_inc(s_aT, 1)
                    project(l, k + 2)
                    if k == 3:
                        pe.wait_ge(s_g, T * (l + 1))
                        for t in range(T):
                            ins = pe.transpose(ps[7][:, 400 + t * NH:400 + (t + 1) * NH], gT[:, t * P:(t + 1) * P], ident[0:NH, 0:NH])
                        ins.then_inc(s_gi, 1)
                        for h in range(NH):
                            ins = pe.matmul(ps[4 + h // 2][:, (h % 2) * SEQ:(h % 2 + 1) * SEQ], SEL[:, h, :], gT[:, :],
                                            start=True, stop=True)
                        ins.then_inc(s_gb, 1)
                    if k < LEVELS:
                        level(l, k)
                    if k >= 9:
                        attn_apply(l, k - 9)
                    if 8 <= k < 11:
                        attn_turn(l, k - 8)
                    if 7 <= k < 10:
                        attn_scores(l, k - 7)
                    if k == 10:
                        pe.wait_ge(s_mc, l + 1)
                        pe.wait_ge(s_lc, LEVELS * (l + 1))
                        for h in range(NH):
                            c, p = h // 2, h % 2
                            r = slice(DH * p, DH * p + DH)
                            ins = pe.matmul(ps[2 + p][:, c * SEQ:(c + 1) * SEQ], MC[r, 2 + c, 0:P], MC[r, c, :],
                                            start=True, stop=True)
                        ins.then_inc(s_qk, 1)
                pe.wait_ge(s_ex, 3 * (l + 1))
                for h in range(NH):
                    c, p = h // 2, h % 2
                    r = slice(DH * p, DH * p + DH)
                    ins = pe.matmul(ps[4 + p][:, c * P:(c + 1) * P], MC[r, 2 + c, P:SEQ], MC[r, c, P:SEQ], start=True, stop=True)
                ins.then_inc(s_qk, 1)
                pe.wait_ge(s_pe, NHALF * (l + 1))
                for h in range(NH):
                    c, p = h // 2, h % 2
                    v = slice(h * DH, (h + 1) * DH)
                    pe.matmul(ps[0][:, h * DH:(h + 1) * DH], SC[:, p, 2 * c, :], HV[:, 0, v], start=True, stop=True)
                    o = ps[0][:, HW + h * DH:HW + (h + 1) * DH]
                    pe.matmul(o, SX[:, p, c, :], HV[:, 0, v], start=True, stop=False)
                    ins = pe.matmul(o, SC[:, p, 2 * c + 1, :], HV[:, 1, v], start=False, stop=True)
                ins.then_inc(s_ho, 1)
                pe.wait_ge(s_w, 4 * (l + 1))
                for t in range(T):
                    for h in range(NH):
                        e = E[:, h // 2, h % 2, :]
                        o = ps[1 + t][:, h * (DH + 1):(h + 1) * (DH + 1)]
                        ins = pe.matmul(o, e[:, t * P:(t + 1) * P], VM[:, 0, h, :], start=True, stop=(t == 0))
                        if t:
                            ins = pe.matmul(o, e[:, SEQ:SEQ + P], VM[:, 1, h, :], start=False, stop=True)
                    ins.then_inc(s_num, 1)
                pe.wait_ge(s_fo, 3 * (l + 1))
                wo = [unit(unit_base[l] + len(SLABS) + n, KD, BANK) for n in range(2)]
                for n in range(2):
                    for t in range(T):
                        for k in range(4, 8):
                            pe.matmul(ps[4 + 2 * n + t][:, :], mixT[:, k, t * P:(t + 1) * P], wo[n][:, k, :],
                                      start=(k == 4), stop=False)
                for t in range(T):
                    pe.wait_ge(s_og, T * l + t + 1)
                    b = ps[3] if t == 0 else ps[0]
                    om = OM[:, t, :, :].rearrange("p h d -> p (h d)")
                    for c in range(4):
                        ins = pe.transpose(b[:, c * P:(c + 1) * P], om[:, c * P:(c + 1) * P], ident[:, :])
                    ins.then_inc(s_mt, 1)
                for n in range(2):
                    for t in range(T):
                        pe.wait_ge(s_me if t == 0 else s_me1, l + 1)
                        for k in range(4):
                            ins = pe.matmul(ps[4 + 2 * n + t][:, :], mixT[:, k, t * P:(t + 1) * P], wo[n][:, k, :],
                                            start=False, stop=(k == 3))
                        ins.then_inc(s_wo, 1)

                if l == DEPTH - 1:
                    pe.wait_ge(s_res, 12)
                    pe.matmul(ps[0][:, 0:2], ident[:, :], UO[:, 0:2], start=True, stop=True).then_inc(s_used, SPLIT)
                turn(2 * l + 1)
                if l == 0:
                    pe.wait_ge(s_hTl, 8)

                    def down(i):
                        pe.wait_ge(s_dwl, i + 1)
                        pe.wait_ge(s_hdl, i + 1)
                        for n in range(2):
                            w = slice(n * BANK, (n + 1) * BANK)
                            for t in range(T):
                                v = slice(t * P, (t + 1) * P)
                                ins = three(ps[4 + 2 * n + t][:, :], HTh[:, i % 2, v], HTl[:, i % 2, v],
                                            dwh[:, i % 2, w], dwl[:, i % 2, w], i == 0, i == NB - 1)
                        ins.then_inc(s_dd, 1)

                    for i in range(NB):
                        if i >= 4:
                            pe.wait_ge(s_ht, i - 3)
                        pe.wait_ge(s_gul, i + 1)
                        for r in range(2):
                            for k in range(KD):
                                ins = three(ps[i % 4][:, r * SEQ:(r + 1) * SEQ], guh[:, i % 2, r, k, :], gul[:, i % 2, r, k, :],
                                            dTh[:, k, :], dTl[:, k, :], k == 0, k == KD - 1)
                        ins.then_inc(s_gu, 1)
                        if i >= 2:
                            down(i - 2)
                    down(NB - 2)
                    down(NB - 1)

            pe.wait_ge(s_rw, 16)
            for t in range(T):
                pe.wait_ge(s_hT, 4 * (2 * DEPTH - 1) + 2 * t + 2)
                for k in range(KD):
                    ins = pe.matmul(ps[7][:, t * NE:(t + 1) * NE], hT[:, k, t * P:(t + 1) * P], RW[:, k, :],
                                    start=(k == 0), stop=(k == KD - 1))
            ins.then_inc(s_lg, 1)
            pe.wait_ge(s_rt, RT_CHOSEN)
            m = [RT[:, 10, t * NE:(t + 1) * NE] for t in range(T)]
            pe.matmul(ps[7][:, 32:40], UO[:, 0:P], m[0], start=True, stop=True)
            pe.matmul(ps[7][:, 40:48], UO[:, P:], m[0], start=True, stop=False)
            pe.matmul(ps[7][:, 40:48], UO[:, 0:P], m[1], start=False, stop=True)
            pe.matmul(ps[7][:, 48:56], UO[:, P:], m[0], start=True, stop=False)
            pe.matmul(ps[7][:, 48:56], UO[:, P:], m[1], start=False, stop=True).then_inc(s_rk, 1)

            def gather(j):
                pe.wait_ge(s_sel, j + 1)
                for b in range(2):
                    for c in range(4):
                        v = slice((4 * b + c) * P, (4 * b + c + 1) * P)
                        for t in range(T):
                            ins = pe.matmul(ps[2 + b][:, c * P:(c + 1) * P], XN[:, t, v], selS[:, t, :],
                                            start=(t == 0), stop=(t == T - 1))
                    ins.then_inc(s_gx, 1)

            def combine(j, i, last=False):
                t, n = i // 2, i % 2
                b = ps[i] if last else ps[7]
                if i == 0:
                    pe.wait_ge(s_yl, 2 * j + 2)
                    pe.wait_ge(s_sTc, j + 1)
                elif not last:
                    pe.wait_ge(s_ca, 4 * j + i)
                st_ = selT[:, t * P:(t + 1) * P]
                pe.matmul(b[:, :], st_, yeh[:, n * BANK:(n + 1) * BANK], start=True, stop=False)
                pe.matmul(b[:, :], st_, yel[:, n * BANK:(n + 1) * BANK], start=False, stop=True).then_inc(s_cz, 1)

            pe.wait_ge(s_xg, T)
            gather(0)
            pe.wait_ge(s_jl, 1)
            njobs = pe.value_load(jobs[0:1, 16:17], min_val=2, max_val=MAXJOBS)
            with pe.Fori(0, njobs) as j:
                def turn_hidden(c):
                    pe.wait_ge(s_eh, NCH * j + c + 1)
                    if c:
                        pe.wait_ge(s_hl, NCH * j + c)
                    for b in range(4):
                        ins = pe.transpose(ps[6][:, b * P:(b + 1) * P], hid[:, c % 2, b * P:(b + 1) * P], ident[:, :])
                    ins.then_inc(s_et, 1)

                for q, (kind, c, h) in enumerate(ORDER):
                    if q == AT["down", NCH - 1, 0]:
                        turn_hidden(NCH - 1)
                        gather(j + 1)
                    if (kind, h) == ("gate", 0):
                        if c == 0:
                            pe.wait_ge(s_xl, 2 * j + 1)
                        elif c >= 2:
                            pe.wait_ge(s_eh, NCH * j + c - 1)
                    if (kind, c, h) == ("gate", 0, 1):
                        pe.wait_ge(s_xl, 2 * j + 2)
                    if (kind, h) == ("down", 0):
                        if c == 0:
                            pe.wait_ge(s_yl, 2 * j + 2)
                        pe.wait_ge(s_hl, NCH * j + c + 1)
                    pe.wait_ge(s_lo, nth_piece(j, q))
                    hi, lo = high[:, q % SPLIT, :], low[:, q % SPLIT, :]
                    if kind == "down":
                        for b in range(2):
                            bb_ = 2 * h + b
                            v = slice(bb_ * P, (bb_ + 1) * P)
                            for n in range(2):
                                w = slice(b * D + n * BANK, b * D + (n + 1) * BANK)
                                ins = three(ps[4 + n][:, :], hdh[:, c % 2, v], hdl[:, c % 2, v], hi[:, w], lo[:, w],
                                            c == 0 and bb_ == 0, c == NCH - 1 and bb_ == 3)
                    else:
                        o = ps[2 * (c % 2) + (kind == "up")][:, :]
                        for k in range(4):
                            w = slice(k * BANK, (k + 1) * BANK)
                            ins = three(o, xeh[:, 4 * h + k, :], xel[:, 4 * h + k, :], hi[:, w], lo[:, w],
                                        h == 0 and k == 0, h == 1 and k == 3)
                    ins.then_inc(s_used, 1)
                    if 1 <= q < 5:
                        combine(j, q - 1)
                    if q == 6:
                        pe.wait_ge(s_ca, 4 * j + 4)
                        pe.wait_ge(s_gc, j + 1)
                        for t in range(T):
                            pe.transpose(ps[7][:, t * P:(t + 1) * P], selS[:, t, :], ident[:, :])
                        for t in range(T):
                            ins = pe.matmul(ps[7][:, SEQ:SEQ + 1], selS[:, t, :], gcol[:, t:t + 1], start=(t == 0), stop=(t == T - 1))
                        ins.then_inc(s_sT, 1)
                    if (kind, h) == ("gate", 1) and c:
                        turn_hidden(c - 1)
            for i in range(4):
                combine(njobs, i, last=True)


_INS = ['x', 'attn_norm', 'w_in', 'hgrn_lb', 'hgrn_norm', 'mlstm_conv', 'mlstm_b_i', 'mlstm_b_f', 'mlstm_norm',
        'fox_b_f', 'w_out', 'ffn_norm', 'dense_w_gate', 'dense_w_up', 'dense_w_down', 'router', 'moe_w_gate',
        'moe_w_up', 'moe_w_down', 'final_norm']


def kernel(**inputs):
    import numpy as _np
    import concourse.bacc as _bacc
    from concourse import mybir as _mybir
    from concourse.bass_utils import run_bass_kernel_spmd as _run

    nc = _bacc.Bacc("TRN2", target_bir_lowering=False, num_devices=1)
    arrays, args = {}, []
    for name in _INS:
        a = _np.ascontiguousarray(inputs[name])
        arrays[f"in_{name}_dram"] = a
        args.append(nc.dram_tensor(f"in_{name}_dram", a.shape, _mybir.dt.from_np(a.dtype), kind="ExternalInput").ap())
    shape = _np.shape(inputs['x'])
    args.append(nc.dram_tensor("out_0_dram", shape, _mybir.dt.from_np(_np.dtype('float32')), kind="ExternalOutput").ap())
    bass_hybrid_trunk_kernel(nc, *args)
    r = _run(nc, [arrays], core_ids=[0])
    return r.results[0]["out_0_dram"]
```
